# Optimizing a Trainium2 kernel written in Bass

```python
import jax, jax.numpy as jnp
from jax import lax
import numpy as np

D_MODEL = 1024
BATCH = 1
SEQ = 512
DEPTH = 2

CHUNK = 128
D_SGU = D_MODEL
SGU_GROUPS = 8
SGU_GC = D_SGU // SGU_GROUPS
D_POOL = D_MODEL
POOL_WINDOWS = (2, 4, 8, 16)
POOL_GROUPS = len(POOL_WINDOWS)
POOL_GC = D_POOL // POOL_GROUPS
D_CONV = D_MODEL
CONV_WIDTH = 31
N_BRANCH = 3
D_FF = -(-8 * D_MODEL // (3 * 256)) * 256
EPS = 1e-6

OFF_U = 0
OFF_V = OFF_U + D_SGU
OFF_POOL = OFF_V + D_SGU
OFF_GLU = OFF_POOL + D_POOL
OFF_GATE = OFF_GLU + 2 * D_CONV
D_IN = OFF_GATE + N_BRANCH * D_MODEL

kernel_name = "hybrid_sgu_pool_conv_adaln_block"

def rmsnorm(x, g):
    xf = x.astype(jnp.float32)
    y = xf * lax.rsqrt(jnp.mean(xf * xf, axis=-1, keepdims=True) + EPS)
    return (y * g.astype(jnp.float32)).astype(x.dtype)

def layernorm(x, g, b):
    xf = x.astype(jnp.float32)
    mu = jnp.mean(xf, axis=-1, keepdims=True)
    var = jnp.mean(jnp.square(xf - mu), axis=-1, keepdims=True)
    y = (xf - mu) * lax.rsqrt(var + EPS) * g.astype(jnp.float32) + b.astype(jnp.float32)
    return y.astype(x.dtype)

def spatial_gating(u, v, ln_g, ln_b, w_s, b_s):
    B, S, _ = v.shape
    v = layernorm(v, ln_g, ln_b)
    vc = v.reshape(B, S // CHUNK, CHUNK, SGU_GROUPS, SGU_GC)
    mask = jnp.tril(jnp.ones((CHUNK, CHUNK), dtype=w_s.dtype))
    w = w_s * mask
    mixed = jnp.einsum('gts,bnsgc->bntgc', w, vc) + jnp.transpose(b_s)[None, None, :, :, None]
    return u * mixed.reshape(B, S, D_SGU)

def multiscale_pool(p, w_pool, pool_scale):
    B, S, _ = p.shape
    pg = p.reshape(B, S, POOL_GROUPS, POOL_GC).astype(jnp.float32)
    cs = jnp.cumsum(pg, axis=1)
    t = jnp.arange(1, S + 1, dtype=jnp.float32)
    outs = []
    for i, win in enumerate(POOL_WINDOWS):
        c_i = cs[:, :, i]
        lag = jnp.pad(c_i, ((0, 0), (win, 0), (0, 0)))[:, :S]
        cnt = jnp.minimum(t, float(win))[None, :, None]
        outs.append((c_i - lag) / cnt - pg[:, :, i])
    pooled = jnp.stack(outs, axis=2).astype(p.dtype)
    y = jnp.einsum('bsgc,gcd->bsgd', pooled, w_pool).reshape(B, S, D_POOL)
    return y * pool_scale

def conformer_conv(a, a_gate, conv_w, conv_b, ln_g, ln_b):
    z = a * jax.nn.sigmoid(a_gate)
    z = lax.conv_general_dilated(
        z, conv_w[:, None, :], window_strides=(1,), padding=[(CONV_WIDTH - 1, 0)],
        dimension_numbers=('NWC', 'WIO', 'NWC'), feature_group_count=D_CONV) + conv_b
    z = layernorm(z, ln_g, ln_b)
    return jax.nn.silu(z)

def setup_inputs(seed: int = 0) -> dict:
    key = jax.random.key(seed)
    ks = jax.random.split(key, 32)
    L, D = DEPTH, D_MODEL

    def nrm(k, shape, scale):
        return jax.random.normal(k, shape, dtype=jnp.float32) * scale

    return {
        "x": nrm(ks[0], (BATCH, SEQ, D), 1.0),
        "c": nrm(ks[1], (BATCH, D), 1.0),
        "w_ada": nrm(ks[2], (L, D, 6 * D), 0.5 * D ** -0.5),
        "b_ada": nrm(ks[3], (L, 6 * D), 0.01),
        "g_mix": 1.0 + nrm(ks[4], (L, D), 0.1),
        "w_in": nrm(ks[5], (L, D, D_IN), D ** -0.5),
        "b_in": nrm(ks[6], (L, D_IN), 0.01),
        "sgu_ln_g": 1.0 + nrm(ks[7], (L, D_SGU), 0.1),
        "sgu_ln_b": nrm(ks[8], (L, D_SGU), 0.01),
        "sgu_w_s": nrm(ks[9], (L, SGU_GROUPS, CHUNK, CHUNK), 0.5 * CHUNK ** -0.5),
        "sgu_b_s": 1.0 + nrm(ks[10], (L, SGU_GROUPS, CHUNK), 0.1),
        "w_pa": nrm(ks[11], (L, D_SGU, D), D_SGU ** -0.5),
        "pool_w": nrm(ks[12], (L, POOL_GROUPS, POOL_GC, POOL_GC), POOL_GC ** -0.5),
        "pool_scale": 1.0 + nrm(ks[13], (L, D_POOL), 0.1),
        "w_pb": nrm(ks[14], (L, D_POOL, D), D_POOL ** -0.5),
        "conv_w": nrm(ks[15], (L, CONV_WIDTH, D_CONV), CONV_WIDTH ** -0.5),
        "conv_b": nrm(ks[16], (L, D_CONV), 0.01),
        "conv_ln_g": 1.0 + nrm(ks[17], (L, D_CONV), 0.1),
        "conv_ln_b": nrm(ks[18], (L, D_CONV), 0.01),
        "w_pc": nrm(ks[19], (L, D_CONV, D), D_CONV ** -0.5),
        "w_out": nrm(ks[20], (L, D, D), D ** -0.5),
        "g_ffn": 1.0 + nrm(ks[21], (L, D), 0.1),
        "w_ffn_in": nrm(ks[22], (L, D, 2 * D_FF), D ** -0.5),
        "w_ffn_out": nrm(ks[23], (L, D_FF, D), D_FF ** -0.5),
        "g_final": 1.0 + nrm(ks[24], (D,), 0.1),
    }

def reference(x, c, w_ada, b_ada, g_mix, w_in, b_in, sgu_ln_g, sgu_ln_b, sgu_w_s, sgu_b_s, w_pa,
              pool_w, pool_scale, w_pb, conv_w, conv_b, conv_ln_g, conv_ln_b, w_pc, w_out,
              g_ffn, w_ffn_in, w_ffn_out, g_final):
    B, S, D = x.shape
    c_act = jax.nn.silu(c)
    for l in range(DEPTH):
        ada = (c_act @ w_ada[l] + b_ada[l])[:, None, :]
        sh_m, sc_m, gt_m, sh_f, sc_f, gt_f = jnp.split(ada, 6, axis=-1)

        h = rmsnorm(x, g_mix[l]) * (1.0 + sc_m) + sh_m
        z = h @ w_in[l] + b_in[l]
        u = jax.nn.gelu(z[..., OFF_U:OFF_V], approximate=False)
        v = jax.nn.gelu(z[..., OFF_V:OFF_POOL], approximate=False)
        p = z[..., OFF_POOL:OFF_GLU]
        a = z[..., OFF_GLU:OFF_GLU + D_CONV]
        a_gate = z[..., OFF_GLU + D_CONV:OFF_GATE]
        gates = jax.nn.sigmoid(z[..., OFF_GATE:]).reshape(B, S, N_BRANCH, D)

        y_a = spatial_gating(u, v, sgu_ln_g[l], sgu_ln_b[l], sgu_w_s[l], sgu_b_s[l]) @ w_pa[l]
        y_b = multiscale_pool(p, pool_w[l], pool_scale[l]) @ w_pb[l]
        y_c = conformer_conv(a, a_gate, conv_w[l], conv_b[l], conv_ln_g[l], conv_ln_b[l]) @ w_pc[l]
        merged = gates[:, :, 0] * y_a + gates[:, :, 1] * y_b + gates[:, :, 2] * y_c
        x = x + gt_m * (merged @ w_out[l])

        h = rmsnorm(x, g_ffn[l]) * (1.0 + sc_f) + sh_f
        gu = h @ w_ffn_in[l]
        g_part, u_part = jnp.split(gu, 2, axis=-1)
        x = x + gt_f * ((jax.nn.silu(g_part) * u_part) @ w_ffn_out[l])
    return rmsnorm(x, g_final)


_drawn_inputs = setup_inputs


def setup_inputs(seed=0):
    import zlib

    import numpy as np

    out = dict(_drawn_inputs(seed))
    spreads = {}
    factors = {'b_ada': 3.554,
     'b_in': 8.0,
     'sgu_ln_g': 8.0,
     'sgu_ln_b': 64.0,
     'sgu_b_s': 3.361,
     'conv_b': 8.0,
     'conv_ln_g': 3.247,
     'conv_ln_b': 42.214,
     'pool_scale': 3.109}
    for name, (base, spread) in spreads.items():
        noise = np.random.default_rng([zlib.crc32(name.encode()), seed]).standard_normal(out[name].shape)
        drawn = base * np.exp(spread * noise) if base else spread * noise
        out[name] = __import__('jax').numpy.asarray(drawn.astype(out[name].dtype))
    for name, factor in factors.items():
        out[name] = (out[name] * factor).astype(out[name].dtype)
    return out
```

```python
import concourse.bass as bass
from concourse import mybir
import numpy as np
from contextlib import ExitStack

P = 128
D = 1024
S = 512
DEPTH = 2
CT = D // P
D_FF = 2816
FT = D_FF // P
TAPS = 31
PAD = TAPS - 1
WINDOWS = (2, 4, 8, 16)
WMAX = max(WINDOWS)
EPS = 1e-6

UC = 1024
UNIT, at = {}, 0
for stage, n in (("V", 8), ("A", 16), ("U", 8), ("BRA", 16), ("P", 8), ("POOL", 2), ("BRB", 16),
                 ("BRC", 16), ("OUT", 8), ("FI", 2 * FT), ("FO", FT)):
    UNIT[stage] = at
    at += n
UNITS = at
RING = 4
RAW = 2

def bases(*counts):
    out, n = {}, 0
    for name, k in counts:
        out[name] = n
        n += k
    return out, n


ACT_EVAC, N_ACT_EVAC = bases(("A", 8), ("U", 8), ("BRA", 8), ("P", 8), ("BRB", 8), ("BRC", 8), ("FI", FT))
DVE_EVAC, N_DVE_EVAC = bases(("V", 8), ("A", 8), ("U", 8), ("BRA", 8), ("BRB", 8), ("BRC", 8), ("OUT", 8), ("FO", 8))
SPLIT, N_SPLIT = bases(("N1", 8), ("U", 8), ("P", 8), ("POOL", 8), ("C", 8), ("BRC", 8), ("N2", 8), ("FI", FT))
SQ, N_SQ = bases(("C", 8), ("OUT", 8), ("FO", 8))
ADA_HALVES = 12
ADA_CHUNKS = 4 * ADA_HALVES

DVE_STEPS = 380

COL, N_COL = bases(("g_mix", 8), ("b_in", 64), ("g_ffn", 8), ("conv_b", 8), ("conv_g", 8), ("conv_lb", 8),
                   ("pool_scale", 8), ("conv_w", 8 * TAPS))
FIX, N_FIX = bases(("b_ada", 48 * DEPTH + 16), ("g_final", 8), ("c", 8), ("eps", 1), ("head", 4 * WMAX),
                   ("ident", P), ("ones", P), ("mean", P))
BT = {"u": 0, "v": 8, "p": 16, "a": 24, "ag": 32, "gate": 40}
GT_M, SH_F, SC_F, GT_F, SH_M, SC_M = (8 * j for j in range(6))


class Sem:

    def __init__(self, handle, per_layer=0, start=0, unit=1):
        self.h, self.per, self.start, self.unit = handle, per_layer, start, unit

    def at(self, layer, n):
        assert not isinstance(n, int) or n + self.start > 0
        return (layer * self.per + (n + self.start)) * self.unit


class Steps:

    def __init__(self, eng, sem):
        self.eng, self.sem, self.layer, self.n, self.loop = eng, sem, 0, 0, None

    def did(self, ins):
        ins.then_inc(self.sem.h, 1)
        self.n += 1

    def settle(self):
        n = self.n if self.loop is None else self.loop + self.n
        self.eng.wait_ge(self.sem.h, self.sem.at(self.layer, n))


def trunk(nc, xT, fixed, cols, rows, ws, w_ada, weights, out):
    f32, f32r = mybir.dt.float32, mybir.dt.float32r
    ALU, ACT = mybir.AluOpType, mybir.ActivationFunctionType
    AX = mybir.AxisListType
    ds = bass.ds

    top = [1152]

    def aligned(n):
        return -(-n // 32) * 32

    def place(name, width, dt=f32, offset=None):
        if offset is None:
            offset = top[0]
            top[0] += aligned(4 * width)
        return nc.alloc_sbuf_tensor_at(name, [P, width], dt, offset=offset), offset

    x, _ = place("x", CT * S)
    raw, _ = place("raw", RAW * UC)
    whi, _ = place("whi", RING * UC, f32r)
    wlo, _ = place("wlo", RING * UC, f32r)
    h_hi, h_at = place("h_hi", CT * S, f32r)
    h_lo, _ = place("h_lo", CT * S, f32r)
    mid_lo, lo_at = place("mid_lo", FT * S, f32r)
    mid_hi, hi_at = place("mid_hi", FT * S, f32r)
    merged, merged_at = place("merged", CT * S)
    ada_raw, _ = place("ada_raw", 2 * UC)
    ada_acc, _ = place("ada_acc", 512)
    atmp, _ = place("atmp", 2 * S)
    dtmp, _ = place("dtmp", 2 * S)
    sq, _ = place("sq", 2 * S)
    ssum, _ = place("ssum", S)
    rstd, _ = place("rstd", S)
    col, _ = place("col", N_COL)
    fix, _ = place("fix", N_FIX)
    ada, _ = place("ada", 48)
    gain, _ = place("gain", CT)
    cact, _ = place("cact", CT)
    vbn, _ = place("vbn", 4 * 2 * 6)
    vmv, _ = place("vmv", 4 * 2)
    vstd, _ = place("vstd", 4)
    FREE = FT - 2 * CT
    OPA, OPB = (FREE, 0), (FREE + CT, CT)
    gap = lo_at + 4 * 2 * CT * S
    assert gap + 4 * 2 * FREE * S == hi_at + 4 * FREE * S
    ZW = PAD + S
    ws_at = gap + aligned(4 * CT * ZW)
    pro_at = ws_at + 4 * 8 * P
    assert pro_at <= gap + 4 * 2 * FREE * S
    zc, _ = place("zc", CT * ZW, offset=gap)
    wsT, _ = place("wsT", 8 * P, offset=ws_at)
    vtok, _ = place("vtok", 4 * D, offset=lo_at + 4 * CT * S)
    PW = WMAX - 1 + S
    ptmp, _ = place("ptmp", 2 * PW, offset=lo_at)
    wsum, _ = place("wsum", 2 * PW, offset=lo_at + aligned(4 * 2 * PW))
    bc, _ = place("bc", 4 * D, offset=merged_at)
    pro_raw = [place(f"pro_raw{h}", 4 * UC, offset=lo_at + 4 * 4 * UC * h if h < 3 else pro_at)[0]
               for h in range(4)]
    pro_acc, _ = place("pro_acc", 4 * 512, offset=h_at)
    psum = nc.alloc_psum_tensor("psum", [P, 8 * 512], f32)

    def bank(b):
        return psum[:, 512 * b:512 * b + 512]

    def tile(t, k, w=S):
        return t[:, k * w:(k + 1) * w]

    def c1(t, k):
        return t[:, k:k + 1]

    ident = fix[:, FIX["ident"]:FIX["ident"] + P]
    ones = fix[:, FIX["ones"]:FIX["ones"] + P]
    mean = fix[:, FIX["mean"]:FIX["mean"] + P]
    eps = c1(fix, FIX["eps"])

    ctx = ExitStack()
    with ctx:
        def sem(name, per_layer=0, start=0, unit=1):
            return Sem(ctx.enter_context(nc.semaphore(name)), per_layer, start, unit)

        fix_in, x_in = sem("fix_in"), sem("x_in")
        pro_in = [sem(f"pro_in{h}") for h in range(4)]
        raw_in = [sem(f"raw_in{s}", UNITS // RAW, unit=16) for s in range(RAW)]
        ada_in = [sem(f"ada_in{s}", ADA_CHUNKS // 2, unit=16) for s in range(2)]
        layer_in = sem("layer_in", 6, unit=16)
        out_done = sem("out_done")
        w_hi_done = sem("w_hi_done", UNITS)
        act_evac = sem("act_evac", N_ACT_EVAC)
        x_hi = sem("x_hi", N_SPLIT)
        sq_ready = sem("sq_ready", N_SQ, 8)
        std_ready = sem("std_ready", 4)
        v_gelu = sem("v_gelu", 8)
        silu_ready = sem("silu_ready", 8)
        c_ready = sem("c_ready")
        w_lo_done = sem("w_lo_done", UNITS, RAW)
        ws_masked = sem("ws_masked", 1)
        unit_done = sem("unit_done", UNITS, RING)
        mixed_ready = sem("mixed_ready", 8)
        stat_ready = sem("stat_ready", 4)
        ada_ready = sem("ada_ready", ADA_HALVES, 4)
        ff_bank = sem("ff_bank", 7)
        dve_evac = sem("dve_evac", N_DVE_EVAC)
        val_ready = sem("val_ready", N_SPLIT)
        x_lo = sem("x_lo", N_SPLIT)
        sq_added = sem("sq_added", N_SQ, 8 + 2)
        zsum_ready = sem("zsum_ready", 1)
        centered = sem("centered", 8)
        vstat_ready = sem("vstat_ready", 4)
        v_ready = sem("v_ready", 4)
        added = sem("added", 8)
        ada_used = sem("ada_used", ADA_CHUNKS, 2)
        ada_read = sem("ada_read", ADA_HALVES, 4)
        pro_acc_ready = sem("pro_acc_ready")
        dve_step = sem("dve_step", DVE_STEPS)
        y_ready = sem("y_ready")

        block = ctx.enter_context(nc.Block())

        @block.sync
        def _(sp):
            sp.dma_start(fix[:, :], fixed[:, :]).then_inc(fix_in.h, 16)
            for h in range(4):
                sp.dma_start(pro_raw[h][:, :].rearrange("p (c n) -> p c n", c=4),
                             w_ada[4 * h:4 * h + 4, :, :].rearrange("c p n -> p c n")).then_inc(pro_in[h].h, 16)
                if h == 0:
                    sp.dma_start(x[:, :], xT[:, :]).then_inc(x_in.h, 16)

            with sp.Fori(0, DEPTH) as layer:
                sp.dma_start(col[:, :], cols[ds(layer, 1), :, :].rearrange("a p n -> p (a n)")).then_inc(layer_in.h, 16)
                for r in range(4):
                    sp.dma_start(tile(bc, r, D), rows[ds(layer * 4 + r, 1), :].to_broadcast([P, D])).then_inc(layer_in.h, 16)
                sp.dma_start(wsT[:, :], ws[ds(layer, 1), :, :].rearrange("a p n -> p (a n)")).then_inc(layer_in.h, 16)

                def load_unit(i, c):
                    sp.wait_ge(w_lo_done.h, w_lo_done.at(layer, i * 4 + (c - RAW + 1)))
                    sp.dma_start(tile(raw, c % RAW, UC), weights[ds(layer * UNITS + (i * 4 + c), 1), :, :]
                                 .rearrange("a p n -> p (a n)")).then_inc(raw_in[c % RAW].h, 16)

                def load_ada(c):
                    i, k, m = c
                    sp.wait_ge(ada_used.h, ada_used.at(layer, i * m + (k - 1)))
                    sp.dma_start(tile(ada_raw, k % 2, UC), w_ada[ds(layer * ADA_CHUNKS + (i * m + (k + 16)), 1), :, :]
                                 .rearrange("a p n -> p (a n)")).then_inc(ada_in[k % 2].h, 16)

                with sp.Fori(0, 16) as i:
                    for c in range(4):
                        load_unit(i, c)
                with sp.Fori(0, 4) as i:
                    for c in range(4):
                        if c % 2 == 0:
                            load_ada((i, c // 2, 2))
                        load_unit(i, 64 + c)
                with sp.Fori(0, 6) as i:
                    for c in range(4):
                        load_ada((i, 8 + c, 4))
                        load_unit(i, 80 + c)
                with sp.Fori(0, 8) as i:
                    for c in range(4):
                        if c % 2 == 0:
                            load_ada((i, 32 + c // 2, 2))
                        load_unit(i, 104 + c)
                with sp.Fori(0, 7) as i:
                    for c in range(4):
                        load_unit(i, 136 + c)

            for k in range(CT):
                sp.wait_ge(y_ready.h, k + 2)
                sp.dma_start(out[:, k * S:(k + 1) * S], tile(x, k)).then_inc(out_done.h, 16)
            sp.wait_ge(out_done.h, 16 * CT)

        @block.gpsimd
        def _(pool):
            pool.sem_inc(w_lo_done.h, RAW)

            with pool.Fori(0, DEPTH) as layer:
                def low_part(i, c):
                    s = c % RING
                    pool.wait_ge(w_hi_done.h, w_hi_done.at(layer, i * 4 + (c + 1)))
                    pool.tensor_tensor(tile(wlo, s, UC), tile(raw, c % RAW, UC), tile(whi, s, UC).bitcast(f32),
                                       ALU.subtract).then_inc(w_lo_done.h, 1)

                for c in range(7):
                    low_part(0, c)
                pool.wait_ge(layer_in.h, layer_in.at(layer, 6))
                low_part(0, 7)
                w3 = wsT[:, :].rearrange("p (g t) -> p g t", g=8)
                pool.affine_select(out=w3, in_=w3, compare_op=ALU.is_ge, fill=0.0, base=0,
                                   pattern=[[0, 8], [1, P]], channel_multiplier=-1).then_inc(ws_masked.h, 1)
                with pool.Fori(0, (UNITS - 8) // 4) as i:
                    for c in range(4):
                        low_part(i, 8 + c)

        @block.scalar
        def _(act):
            A = nc.scalar.activation

            act.wait_ge(fix_in.h, 16)
            A(cact[:, :], fix[:, FIX["c"]:FIX["c"] + CT], ACT.Silu).then_inc(c_ready.h, 1)
            act.wait_ge(x_in.h, 16)
            for k in range(CT):
                if k >= 2:
                    act.wait_ge(sq_added.h, k + 1)
                A(tile(sq, k % 2), tile(x, k), ACT.Square).then_inc(sq_ready.h, 1)

            with act.Fori(0, DEPTH) as layer:
                def weight_hi(i, c):
                    act.wait_ge(raw_in[c % RAW].h, raw_in[c % RAW].at(layer, i * 2 + (c // 2 + 1)))
                    act.wait_ge(unit_done.h, unit_done.at(layer, i * 4 + (c - RING + 1)))
                    nc.scalar.copy(tile(whi, c % RING, UC), tile(raw, c % RAW, UC)).then_inc(w_hi_done.h, 1)

                def unit_is_done(i, c):
                    act.wait_ge(unit_done.h, unit_done.at(layer, i * 4 + (c + 1)))

                def split_hi(hi, t, stage, k):
                    act.wait_ge(val_ready.h, val_ready.at(layer, SPLIT[stage] + k + 1))
                    nc.scalar.copy(tile(hi, t), tile(dtmp, k % 2)).then_inc(x_hi.h, 1)

                def norm(n, which, shift, stage):
                    act.wait_ge(stat_ready.h, stat_ready.at(layer, n + 1))
                    A(rstd[:, :], bank(6), ACT.Sqrt, bias=eps).then_inc(std_ready.h, 1)
                    for k in range(CT):
                        act.wait_ge(val_ready.h, val_ready.at(layer, SPLIT[stage] + k + 1))
                        A(tile(h_hi, k), tile(dtmp, k % 2), ACT.Identity, bias=c1(ada, shift + k)).then_inc(x_hi.h, 1)

                def square(src, stage, k):
                    act.wait_ge(sq_added.h, sq_added.at(layer, SQ[stage] + k - 1))
                    A(tile(sq, k % 2), src, ACT.Square).then_inc(sq_ready.h, 1)

                for c in range(3):
                    weight_hi(0, c)
                norm(0, "g_mix", SH_M, "N1")
                weight_hi(0, 3)

                act.wait_ge(layer_in.h, layer_in.at(layer, 6))
                for u in range(8):
                    weight_hi(0, u + 4)
                    if u % 4 == 3:
                        for tt in range(4):
                            n = u // 4 * 4 + tt
                            v = vtok[:, tt * D + u // 4 * 512:tt * D + u // 4 * 512 + 512]
                            act.wait_ge(dve_evac.h, dve_evac.at(layer, DVE_EVAC["V"] + n + 1))
                            A(v, v, ACT.Gelu).then_inc(v_gelu.h, 1)

                for p in range(8):
                    u = UNIT["A"] + 2 * p
                    unit_is_done(0, u)
                    if p >= 2:
                        act.wait_ge(dve_evac.h, dve_evac.at(layer, DVE_EVAC["A"] + p - 1))
                    A(tile(atmp, p % 2), bank(u % 4), ACT.Sigmoid, bias=c1(col, COL["b_in"] + BT["ag"] + p)).then_inc(act_evac.h, 1)
                    weight_hi(0, u + 4)
                    weight_hi(0, u + 5)
                    if p == 0:
                        act.wait_ge(vstat_ready.h, vstat_ready.at(layer, 4))
                        A(vstd[:, :].rearrange("p (t a) -> p t a", a=1), vmv[:, :].rearrange("p (t a) -> p t a", a=2)[:, :, 1:2], ACT.Sqrt, bias=eps).then_inc(std_ready.h, 1)

                for g in range(8):
                    u = UNIT["U"] + g
                    unit_is_done(0, u)
                    if g < 2:
                        act.wait_ge(dve_evac.h, dve_evac.at(layer, DVE_EVAC["A"] + 7 + g))
                    else:
                        act.wait_ge(val_ready.h, val_ready.at(layer, SPLIT["U"] + g - 1))
                    A(tile(atmp, g % 2), bank(u % 4), ACT.Gelu, bias=c1(col, COL["b_in"] + BT["u"] + g)).then_inc(act_evac.h, 1)
                    weight_hi(0, u + 4)
                    split_hi(mid_hi, OPA[0] + g, "U", g)

                def gate(branch, stage, n):
                    A(tile(atmp, n % 2), bank((UNIT[stage] + 2 * n) % 4), ACT.Sigmoid,
                      bias=c1(col, COL["b_in"] + BT["gate"] + 8 * branch + n)).then_inc(act_evac.h, 1)

                for n in range(8):
                    u = UNIT["BRA"] + 2 * n
                    unit_is_done(0, u)
                    if n < 2:
                        act.wait_ge(val_ready.h, val_ready.at(layer, SPLIT["U"] + 7 + n))
                    else:
                        act.wait_ge(dve_evac.h, dve_evac.at(layer, DVE_EVAC["BRA"] + n - 1))
                    gate(0, "BRA", n)
                    weight_hi(0, u + 4)
                    weight_hi(0, u + 5)

                for k in range(8):
                    u = UNIT["P"] + k
                    unit_is_done(0, u)
                    if k >= 2:
                        act.wait_ge(val_ready.h, val_ready.at(layer, SPLIT["P"] + k - 1))
                    A(ptmp[:, k % 2 * PW + WMAX - 1:(k % 2 + 1) * PW], bank(u % 4), ACT.Identity,
                      bias=c1(col, COL["b_in"] + BT["p"] + k)).then_inc(act_evac.h, 1)
                    weight_hi(0, u + 4)
                    split_hi(mid_hi, OPB[0] + k, "P", k)

                for q in range(2):
                    weight_hi(0, UNIT["POOL"] + q + 4)
                    for k in range(4 * q, 4 * q + 4):
                        split_hi(mid_hi, OPB[0] + k, "POOL", k)

                for n in range(8):
                    u = UNIT["BRB"] + 2 * n
                    unit_is_done(0, u)
                    if n < 2:
                        act.wait_ge(dve_evac.h, dve_evac.at(layer, DVE_EVAC["BRA"] + 7 + n))
                    else:
                        act.wait_ge(added.h, added.at(layer, n - 1))
                    gate(1, "BRB", n)
                    weight_hi(0, u + 4)
                    if n == 4:
                        weight_hi(0, u + 5)
                        for k in range(CT):
                            act.wait_ge(centered.h, centered.at(layer, k + 1))
                            square(zc[:, k * ZW + PAD:(k + 1) * ZW], "C", k)
                    elif n >= 6:
                        if n == 6:
                            act.wait_ge(stat_ready.h, stat_ready.at(layer, 3))
                            A(rstd[:, :], bank(6), ACT.Sqrt, bias=eps).then_inc(std_ready.h, 1)
                        for k in range(4 * (n - 6), 4 * (n - 6) + 4):
                            act.wait_ge(val_ready.h, val_ready.at(layer, SPLIT["C"] + k + 1))
                            if k >= 2:
                                act.wait_ge(x_lo.h, x_lo.at(layer, SPLIT["C"] + k - 1))
                            A(tile(sq, k % 2), tile(dtmp, k % 2), ACT.Silu, bias=c1(col, COL["conv_lb"] + k)).then_inc(silu_ready.h, 1)
                            act.wait_ge(silu_ready.h, silu_ready.at(layer, k + 1))
                            nc.scalar.copy(tile(mid_hi, OPA[0] + k), tile(sq, k % 2)).then_inc(x_hi.h, 1)
                        weight_hi(0, u + 5)
                    else:
                        weight_hi(0, u + 5)

                for n in range(8):
                    u = UNIT["BRC"] + 2 * n
                    unit_is_done(0, u)
                    if n < 2:
                        act.wait_ge(added.h, added.at(layer, 7 + n))
                    else:
                        act.wait_ge(val_ready.h, val_ready.at(layer, SPLIT["BRC"] + n - 1))
                    gate(2, "BRC", n)
                    weight_hi(0, u + 4)
                    split_hi(mid_hi, OPB[0] + n, "BRC", n)
                    weight_hi(0, u + 5)

                for n in range(8):
                    weight_hi(0, UNIT["OUT"] + n + 4)
                    act.wait_ge(dve_evac.h, dve_evac.at(layer, DVE_EVAC["OUT"] + n + 1))
                    square(tile(x, n), "OUT", n)

                norm(3, "g_ffn", SH_F, "N2")

                with act.Fori(0, FT // 2) as i:
                    for k in range(2):
                        c = UNIT["FI"] + 2 * k
                        unit_is_done(i, c)
                        act.wait_ge(val_ready.h, val_ready.at(layer, i * 2 + (SPLIT["FI"] + k - 1)))
                        A(tile(atmp, k), bank(c % 4), ACT.Silu).then_inc(act_evac.h, 1)
                        weight_hi(i, c + 4)
                        act.wait_ge(val_ready.h, val_ready.at(layer, i * 2 + (SPLIT["FI"] + k + 1)))
                        nc.scalar.copy(mid_hi[:, ds((i * 2 + k) * S, S)], tile(dtmp, k)).then_inc(x_hi.h, 1)
                        weight_hi(i, c + 5)

                for c in range(146, 148):
                    weight_hi(0, c)
                with act.Fori(0, 4) as i:
                    for c in range(4):
                        weight_hi(i, 148 + c)
                for n in range(8):
                    act.wait_ge(dve_evac.h, dve_evac.at(layer, DVE_EVAC["FO"] + n + 1))
                    square(tile(x, n), "FO", n)

            act.wait_ge(stat_ready.h, stat_ready.at(DEPTH, 1))
            A(rstd[:, :], bank(6), ACT.Sqrt, bias=eps).then_inc(std_ready.h, 1)

        @block.vector
        def _(dve):
            V = nc.vector
            steps = Steps(dve, dve_step)

            def did(ins):
                steps.did(ins)

            def then(ins):
                steps.did(ins)
                steps.settle()

            def add_square(layer, stage, k, first=False):
                n = k - CT if stage is None else SQ[stage] + k
                dve.wait_ge(sq_ready.h, sq_ready.at(layer, n + 1))
                if k == 0:
                    V.tensor_copy(ssum[:, :], tile(sq, 0)).then_inc(sq_added.h, 1)
                else:
                    dve.wait_ge(sq_added.h, sq_added.at(layer, n))
                    V.tensor_tensor(ssum[:, :], ssum[:, :], tile(sq, k % 2), ALU.add).then_inc(sq_added.h, 1)

            def ada_finish(scratch, layer, n, at_col, bias_at, settle=True):
                dve.wait_ge(ada_ready.h, ada_ready.at(layer, n + 1))
                r3 = scratch.rearrange("p (c n) -> p c n", c=4)
                V.tensor_tensor(r3, bank(4).rearrange("p (c n) -> p c n", c=4),
                                ident.rearrange("p (a n) -> p a n", a=1).to_broadcast([P, 4, P]), ALU.mult).then_inc(ada_read.h, 1)
                dve.wait_ge(ada_read.h, ada_read.at(layer, n + 1))
                then(V.reduce_sum(ada[:, ds(at_col, 4)], r3, AX.X))
                did(V.tensor_tensor(ada[:, ds(at_col, 4)], ada[:, ds(at_col, 4)], fix[:, ds(bias_at, 4)], ALU.add))
                if settle:
                    steps.settle()

            dve.wait_ge(fix_in.h, 16)
            dve.sem_inc(sq_added.h, 2)
            dve.sem_inc(ada_used.h, 2)
            dve.wait_ge(c_ready.h, 1)
            for h in range(4):
                dve.wait_ge(pro_in[h].h, 16)
                acc = tile(pro_acc, h)
                for k in range(CT):
                    w = tile(pro_raw[h], k)
                    if k == 0:
                        then(V.tensor_scalar(acc, w, c1(cact, k), None, ALU.mult))
                    elif k < CT - 1:
                        then(V.scalar_tensor_tensor(out=acc, in0=w, scalar=c1(cact, k), in1=acc, op0=ALU.mult, op1=ALU.add))
                    else:
                        V.scalar_tensor_tensor(out=acc, in0=w, scalar=c1(cact, k), in1=acc,
                                               op0=ALU.mult, op1=ALU.add).then_inc(pro_acc_ready.h, 1)
                for k in (2 * h, 2 * h + 1):
                    add_square(0, None, k)
                if h:
                    ada_finish(tile(atmp, 0), 0, h - 1 - 4, SH_M + 4 * (h - 1), FIX["b_ada"] + 4 * (h - 1))
            ada_finish(tile(atmp, 0), 0, -1, SH_M + 12, FIX["b_ada"] + 12)
            dve_step.start = steps.n
            steps.n = 0

            with dve.Fori(0, DEPTH) as layer:
                steps.layer = layer

                def unit_is_done(i, c):
                    dve.wait_ge(unit_done.h, unit_done.at(layer, i * 4 + (c + 1)))

                def split_lo(val, hi, lo, stage, k):
                    dve.wait_ge(x_hi.h, x_hi.at(layer, SPLIT[stage] + k + 1))
                    V.tensor_tensor(lo, val, hi.bitcast(f32), ALU.subtract).then_inc(x_lo.h, 1)

                def slot_is_split(stage, k):
                    if SPLIT[stage] + k >= 2:
                        dve.wait_ge(x_lo.h, x_lo.at(layer, SPLIT[stage] + k - 1))

                def ada_chunk(i, k, m):
                    dve.wait_ge(ada_in[k % 2].h, ada_in[k % 2].at(layer, i * (m // 2) + (k // 2 + 1)))
                    w0, w1 = (ada_raw[:, k % 2 * UC + 512 * j:k % 2 * UC + 512 * (j + 1)] for j in range(2))
                    kt = 2 * (k % 4)
                    if k % 4 == 0:
                        then(V.tensor_scalar(ada_acc[:, :], w0, c1(cact, kt), None, ALU.mult))
                    else:
                        dve.wait_ge(ada_used.h, ada_used.at(layer, i * m + k))
                        then(V.scalar_tensor_tensor(out=ada_acc[:, :], in0=w0, scalar=c1(cact, kt), in1=ada_acc[:, :],
                                                    op0=ALU.mult, op1=ALU.add))
                    V.scalar_tensor_tensor(out=ada_acc[:, :], in0=w1, scalar=c1(cact, kt + 1), in1=ada_acc[:, :],
                                           op0=ALU.mult, op1=ALU.add).then_inc(ada_used.h, 1)

                def finish(n, settle=True):
                    ada_finish(rstd[:, :], layer, n, 4 * n, layer * 48 + (FIX["b_ada"] + 16 + 4 * n), settle)

                def gains(g, scale):
                    then(V.tensor_scalar(gain[:, :], ada[:, scale:scale + CT], 1.0, None, ALU.add))
                    then(V.tensor_tensor(gain[:, :], gain[:, :], g, ALU.mult))

                def norm(n, g, scale, shift, stage):
                    gains(g, scale)
                    dve.wait_ge(std_ready.h, std_ready.at(layer, n + 1))
                    then(V.reciprocal(rstd[:, :], rstd[:, :]))

                    def low(k):
                        dve.wait_ge(x_hi.h, x_hi.at(layer, SPLIT[stage] + k + 1))
                        V.scalar_tensor_tensor(out=tile(h_lo, k), in0=tile(dtmp, k % 2), scalar=c1(ada, shift + k),
                                               in1=tile(h_hi, k).bitcast(f32), op0=ALU.add, op1=ALU.subtract).then_inc(x_lo.h, 1)
                    for k in range(CT):
                        if k >= 2:
                            low(k - 2)
                            slot_is_split(stage, k)
                        V.scalar_tensor_tensor(out=tile(dtmp, k % 2), in0=tile(x, k), scalar=c1(gain, k), in1=rstd[:, :],
                                               op0=ALU.mult, op1=ALU.mult).then_inc(val_ready.h, 1)
                    low(CT - 2)
                    low(CT - 1)

                def conv_taps(first, last):
                    for n in range(first, last):
                        j, k = divmod(n, TAPS)
                        z = zc[:, j * ZW + k:j * ZW + k + S]
                        w = c1(col, COL["conv_w"] + j * TAPS + k)
                        if k == 0:
                            then(V.tensor_scalar(bank(7), z, w, c1(col, COL["conv_b"] + j), ALU.mult, ALU.add))
                        elif k < TAPS - 1:
                            then(V.scalar_tensor_tensor(out=bank(7), in0=z, scalar=w, in1=bank(7), op0=ALU.mult, op1=ALU.add))
                        else:
                            then(V.scalar_tensor_tensor(out=z, in0=z, scalar=w, in1=bank(7), op0=ALU.mult, op1=ALU.add))
                            if j == 1:
                                did(V.tensor_tensor(ssum[:, :], zc[:, PAD:ZW], z, ALU.add))
                            elif 1 < j < CT - 1:
                                did(V.tensor_tensor(ssum[:, :], ssum[:, :], z, ALU.add))
                            elif j == CT - 1:
                                V.tensor_tensor(ssum[:, :], ssum[:, :], z, ALU.add).then_inc(zsum_ready.h, 1)

                dve.wait_ge(layer_in.h, layer_in.at(layer, 6))
                norm(0, col[:, COL["g_mix"]:COL["g_mix"] + CT], SC_M, SH_M, "N1")
                z3 = zc[:, :].rearrange("p (j t) -> p j t", j=CT)
                for half in range(2):
                    unit_is_done(0, 4 * half + 3)
                    for tt in range(4):
                        V.tensor_tensor(vtok[:, tt * D + half * 512:tt * D + half * 512 + 512], bank(4 * half + tt),
                                        bc[:, half * 512:half * 512 + 512], ALU.add).then_inc(dve_evac.h, 1)
                for tt in range(4):
                    for half in range(2):
                        dve.wait_ge(v_gelu.h, v_gelu.at(layer, 4 * half + tt + 1))
                        did(V.bn_stats(vbn[:, (2 * tt + half) * 6:(2 * tt + half + 1) * 6],
                                       vtok[:, tt * D + half * 512:tt * D + half * 512 + 512]))
                steps.settle()
                did(V.memset(z3[:, :, 0:PAD], 0.0))
                for tt in range(4):
                    V.bn_aggr(vmv[:, 2 * tt:2 * tt + 2], vbn[:, 12 * tt:12 * tt + 12]).then_inc(vstat_ready.h, 1)

                for p in range(8):
                    u = UNIT["A"] + 2 * p
                    dve.wait_ge(act_evac.h, act_evac.at(layer, ACT_EVAC["A"] + p + 1))
                    unit_is_done(0, u + 1)
                    V.scalar_tensor_tensor(out=z3[:, p, PAD:ZW], in0=bank((u + 1) % 4), scalar=c1(col, COL["b_in"] + BT["a"] + p),
                                           in1=tile(atmp, p % 2), op0=ALU.add, op1=ALU.mult).then_inc(dve_evac.h, 1)
                    if p == 1:
                        dve.wait_ge(std_ready.h, std_ready.at(layer, 2))
                        then(V.reciprocal(vstd[:, :], vstd[:, :]))
                    if p in (1, 2):
                        for tt in (2 * p - 2, 2 * p - 1):
                            v = vtok[:, tt * D:(tt + 1) * D]
                            then(V.tensor_scalar(v, v, c1(vmv, 2 * tt), c1(vstd, tt), ALU.subtract, ALU.mult))
                            then(V.tensor_tensor(v, v, bc[:, D:2 * D], ALU.mult))
                            V.tensor_tensor(v, v, bc[:, 2 * D:3 * D], ALU.add).then_inc(v_ready.h, 1)
                    if p >= 3:
                        dve.wait_ge(dve_evac.h, dve_evac.at(layer, DVE_EVAC["A"] + p + 1))
                        conv_taps(13 * (p - 3), 13 * (p - 2))

                for g in range(8):
                    dve.wait_ge(mixed_ready.h, mixed_ready.at(layer, g + 1))
                    b_s = bc[:, 3 * D + g * P:3 * D + (g + 1) * P].rearrange("p (a t) -> p a t", a=1).to_broadcast([P, 4, P])
                    V.tensor_tensor(tile(sq, g % 2).rearrange("p (n t) -> p n t", n=4),
                                    bank(4 + g % 2).rearrange("p (n t) -> p n t", n=4), b_s, ALU.add).then_inc(dve_evac.h, 1)
                    dve.wait_ge(act_evac.h, act_evac.at(layer, ACT_EVAC["U"] + g + 1))
                    dve.wait_ge(dve_evac.h, dve_evac.at(layer, DVE_EVAC["U"] + g + 1))
                    slot_is_split("U", g)
                    V.tensor_tensor(tile(dtmp, g % 2), tile(sq, g % 2), tile(atmp, g % 2), ALU.mult).then_inc(val_ready.h, 1)
                    conv_taps(65 + 6 * g, 65 + 6 * (g + 1))
                    split_lo(tile(dtmp, g % 2), tile(mid_hi, OPA[0] + g), tile(mid_lo, OPA[1] + g), "U", g)

                for n in range(8):
                    u = UNIT["BRA"] + 2 * n
                    dve.wait_ge(act_evac.h, act_evac.at(layer, ACT_EVAC["BRA"] + n + 1))
                    unit_is_done(0, u + 1)
                    V.tensor_tensor(tile(merged, n), bank((u + 1) % 4), tile(atmp, n % 2), ALU.mult).then_inc(dve_evac.h, 1)
                    conv_taps(113 + 12 * n, 113 + 12 * (n + 1))

                then(V.memset(ptmp[:, :].rearrange("p (a t) -> p a t", a=2)[:, :, 0:WMAX - 1], 0.0))
                for k in range(8):
                    win = WINDOWS[k // 2]
                    src = ptmp[:, k % 2 * PW:(k % 2 + 1) * PW]
                    dve.wait_ge(act_evac.h, act_evac.at(layer, ACT_EVAC["P"] + k + 1))
                    have, span, b = src, 1, 0
                    while span < win:
                        span *= 2
                        lo = WMAX - 1 - (win - span)
                        nxt = wsum[:, b * PW:(b + 1) * PW]
                        then(V.tensor_tensor(nxt[:, lo:PW], have[:, lo:PW], have[:, lo - span // 2:PW - span // 2], ALU.add))
                        have, b = nxt, 1 - b
                    head = have[:, WMAX - 1:WMAX - 1 + WMAX]
                    hd = FIX["head"] + k // 2 * WMAX
                    then(V.tensor_tensor(head, head, fix[:, hd:hd + WMAX], ALU.mult))
                    slot_is_split("P", k)
                    V.scalar_tensor_tensor(out=tile(dtmp, k % 2), in0=have[:, WMAX - 1:PW], scalar=1.0 / win,
                                           in1=src[:, WMAX - 1:PW], op0=ALU.mult, op1=ALU.subtract).then_inc(val_ready.h, 1)
                    conv_taps(209 + 3 * k, 209 + 3 * (k + 1))
                    split_lo(tile(dtmp, k % 2), tile(mid_hi, OPB[0] + k), tile(mid_lo, OPB[1] + k), "P", k)

                for k in range(8):
                    unit_is_done(0, UNIT["POOL"] + k // 4)
                    if k >= 2:
                        split_lo(tile(dtmp, k % 2), tile(mid_hi, OPB[0] + k - 2), tile(mid_lo, OPB[1] + k - 2), "POOL", k - 2)
                    slot_is_split("POOL", k)
                    V.tensor_scalar(tile(dtmp, k % 2), bank(k % 7), c1(col, COL["pool_scale"] + k), None,
                                    ALU.mult).then_inc(val_ready.h, 1)
                for k in (6, 7):
                    split_lo(tile(dtmp, k % 2), tile(mid_hi, OPB[0] + k), tile(mid_lo, OPB[1] + k), "POOL", k)

                for n in range(8):
                    def branch_b():
                        u = UNIT["BRB"] + 2 * n
                        dve.wait_ge(act_evac.h, act_evac.at(layer, ACT_EVAC["BRB"] + n + 1))
                        unit_is_done(0, u + 1)
                        V.tensor_tensor(tile(atmp, n % 2), bank((u + 1) % 4), tile(atmp, n % 2), ALU.mult).then_inc(dve_evac.h, 1)
                        dve.wait_ge(dve_evac.h, dve_evac.at(layer, DVE_EVAC["BRB"] + n + 1))
                        V.tensor_tensor(tile(merged, n), tile(merged, n), tile(atmp, n % 2), ALU.add).then_inc(added.h, 1)
                        if n == 4:
                            finish(0)
                        ada_chunk(0, n, 8)

                    if n < 6:
                        branch_b()
                    if n < 4:
                        conv_taps(233 + 4 * n, min(233 + 4 * (n + 1), CT * TAPS))
                    if n == 4:
                        dve.wait_ge(stat_ready.h, stat_ready.at(layer, 2))
                        for k in range(CT + 2):
                            if k < CT:
                                V.tensor_tensor(z3[:, k, PAD:ZW], z3[:, k, PAD:ZW], bank(6), ALU.subtract).then_inc(centered.h, 1)
                            if k >= 2:
                                add_square(layer, "C", k - 2)
                    if n >= 6:
                        if n == 6:
                            dve.wait_ge(std_ready.h, std_ready.at(layer, 3))
                            then(V.reciprocal(rstd[:, :], rstd[:, :]))
                        for k in range(4 * (n - 6), 4 * (n - 6) + 4 + 2 * (n - 6)):
                            if k >= 2:
                                split_lo(tile(sq, k % 2), tile(mid_hi, OPA[0] + k - 2), tile(mid_lo, OPA[1] + k - 2), "C", k - 2)
                            if k < CT:
                                V.scalar_tensor_tensor(out=tile(dtmp, k % 2), in0=z3[:, k, PAD:ZW], scalar=c1(col, COL["conv_g"] + k),
                                                       in1=rstd[:, :], op0=ALU.mult, op1=ALU.mult).then_inc(val_ready.h, 1)
                        branch_b()

                for n in range(8):
                    u = UNIT["BRC"] + 2 * n
                    if n % 2 == 0:
                        finish(1 + n // 2)
                    ada_chunk(0, 8 + 2 * n, 48)
                    dve.wait_ge(act_evac.h, act_evac.at(layer, ACT_EVAC["BRC"] + n + 1))
                    unit_is_done(0, u + 1)
                    V.tensor_tensor(tile(atmp, n % 2), bank((u + 1) % 4), tile(atmp, n % 2), ALU.mult).then_inc(dve_evac.h, 1)
                    dve.wait_ge(dve_evac.h, dve_evac.at(layer, DVE_EVAC["BRC"] + n + 1))
                    slot_is_split("BRC", n)
                    V.tensor_tensor(tile(dtmp, n % 2), tile(merged, n), tile(atmp, n % 2), ALU.add).then_inc(val_ready.h, 1)
                    split_lo(tile(dtmp, n % 2), tile(mid_hi, OPB[0] + n), tile(mid_lo, OPB[1] + n), "BRC", n)
                    ada_chunk(0, 9 + 2 * n, 48)

                for n in range(8):
                    u = UNIT["OUT"] + n
                    if n % 4 == 0:
                        finish(5 + n // 4)
                    unit_is_done(0, u)
                    V.scalar_tensor_tensor(out=tile(x, n), in0=bank(u % 4), scalar=c1(ada, GT_M + n), in1=tile(x, n),
                                           op0=ALU.mult, op1=ALU.add).then_inc(dve_evac.h, 1)
                    ada_chunk(0, 24 + n, 48)
                    add_square(layer, "OUT", n)

                norm(3, col[:, COL["g_ffn"]:COL["g_ffn"] + CT], SC_F, SH_F, "N2")

                def ffn_pair(i, k, m):
                    c = UNIT["FI"] + 2 * k
                    dve.wait_ge(act_evac.h, act_evac.at(layer, i * m + (ACT_EVAC["FI"] + k + 1)))
                    dve.wait_ge(unit_done.h, unit_done.at(layer, i * (2 * m) + (c + 2)))
                    dve.wait_ge(x_lo.h, x_lo.at(layer, i * m + (SPLIT["FI"] + k - 1)))
                    V.tensor_tensor(tile(dtmp, k % 2), bank((c + 1) % 4), tile(atmp, k % 2), ALU.mult).then_inc(val_ready.h, 1)
                    dve.wait_ge(x_hi.h, x_hi.at(layer, i * m + (SPLIT["FI"] + k + 1)))
                    V.tensor_tensor(mid_lo[:, ds((i * m + k) * S, S)], tile(dtmp, k % 2),
                                    mid_hi[:, ds((i * m + k) * S, S)].bitcast(f32), ALU.subtract).then_inc(x_lo.h, 1)

                with dve.Fori(0, 4) as i:
                    steps.loop, inside = i * 6, steps.n
                    n = 7
                    ada_finish(rstd[:, :], layer, i + n, i * 4 + 4 * n, layer * 48 + (i * 4 + (FIX["b_ada"] + 16 + 4 * n)))
                    for k in range(4):
                        ada_chunk(i, 32 + k, 4)
                        ffn_pair(i, k, 4)
                    assert steps.n - inside == 6
                    steps.loop, steps.n = None, inside + 4 * 6
                finish(11, settle=False)
                with dve.Fori(0, 3) as i:
                    for k in range(2):
                        ffn_pair(i, 16 + k, 2)

                steps.settle()
                for n in range(8):
                    if n < 7:
                        dve.wait_ge(ff_bank.h, ff_bank.at(layer, n + 1))
                    else:
                        unit_is_done(0, UNITS - 1)
                    V.scalar_tensor_tensor(out=tile(x, n), in0=bank(n), scalar=c1(ada, GT_F + n), in1=tile(x, n),
                                           op0=ALU.mult, op1=ALU.add).then_inc(dve_evac.h, 1)
                    if n:
                        add_square(layer, "FO", n - 1)
                add_square(layer, "FO", 7)
                assert steps.n == DVE_STEPS, steps.n

            dve.wait_ge(std_ready.h, std_ready.at(DEPTH, 1))
            V.reciprocal(rstd[:, :], rstd[:, :]).then_inc(y_ready.h, 1)
            dve.wait_ge(y_ready.h, 1)
            for k in range(CT):
                V.scalar_tensor_tensor(out=tile(x, k), in0=tile(x, k), scalar=c1(fix, FIX["g_final"] + k), in1=rstd[:, :],
                                       op0=ALU.mult, op1=ALU.mult).then_inc(y_ready.h, 1)

        @block.tensor
        def _(pe):
            pe.sem_inc(unit_done.h, RING)
            pe.wait_ge(fix_in.h, 16)

            def ada_sum(layer, n, acc):
                pe.wait_ge(ada_read.h, ada_read.at(layer, n)) if not (isinstance(n, int) and n == -4) else None
                pe.matmul(bank(4), ones, acc, start=True, stop=True).then_inc(ada_ready.h, 1)

            for h in range(4):
                pe.wait_ge(pro_acc_ready.h, h + 1)
                ada_sum(0, h - 4, tile(pro_acc, h))

            with pe.Fori(0, DEPTH) as layer:
                def unit_is_split(i, c):
                    pe.wait_ge(w_lo_done.h, w_lo_done.at(layer, i * 4 + (c + 1)))

                def passes(hi, lo, whi_, wlo_, stationary):
                    for a, b in ((hi, whi_), (lo, whi_), (hi, wlo_)):
                        yield (a, b) if stationary else (b, a)

                def unit(i, c, operand, b=None, free=None, tiles=None):
                    s = c % RING
                    b = s if b is None else b
                    if free:
                        pe.wait_ge(free[0].h, free[0].at(layer, free[1]))
                    unit_is_split(i, c)
                    hi, lo, th, tl = operand
                    for kt in range(8):
                        if tiles:
                            pe.wait_ge(x_lo.h, x_lo.at(layer, tiles + kt + 1))
                        w = slice(s * UC + kt * P, s * UC + (kt + 1) * P)
                        for j, (st, mv) in enumerate(passes(tile(hi, th + kt), tile(lo, tl + kt), whi[:, w], wlo[:, w], False)):
                            mm = pe.matmul(bank(b), st, mv, start=(kt == 0 and j == 0), stop=(kt == 7 and j == 2))
                    mm.then_inc(unit_done.h, 1)

                H = (h_hi, h_lo, 0, 0)
                opa = (mid_hi, mid_lo, *OPA)
                opb = (mid_hi, mid_lo, *OPB)

                def channel_sum(wait, n):
                    pe.wait_ge(wait.h, n)
                    pe.matmul(bank(6), mean, ssum[:, :], start=True, stop=True).then_inc(stat_ready.h, 1)

                channel_sum(sq_added, sq_added.at(layer, 0))

                for half in range(2):
                    for q in range(4):
                        c = 4 * half + q
                        unit_is_split(0, c)
                        for j in range(2):
                            kt = 2 * q + j
                            if half == 0:
                                pe.wait_ge(x_lo.h, x_lo.at(layer, SPLIT["N1"] + kt + 1))
                            w = slice(q * UC + j * 512, q * UC + (j + 1) * 512)
                            for tt in range(4):
                                t = slice(kt * S + tt * P, kt * S + (tt + 1) * P)
                                for m, (st, mv) in enumerate(passes(h_hi[:, t], h_lo[:, t], whi[:, w], wlo[:, w], True)):
                                    mm = pe.matmul(bank(4 * half + tt), st, mv, start=(kt == 0 and m == 0), stop=(kt == 7 and m == 2))
                        mm.then_inc(unit_done.h, 1)

                for c in range(4):
                    unit(0, UNIT["A"] + c, H, free=(dve_evac, DVE_EVAC["V"] + c + 1))
                with pe.Fori(0, 3) as i:
                    for c in range(4):
                        f = (act_evac, i * 2 + (ACT_EVAC["A"] + c // 2 + 1)) if c % 2 == 0 else (dve_evac, i * 2 + (DVE_EVAC["A"] + c // 2 + 1))
                        unit(i, UNIT["A"] + 4 + c, H, free=f)

                pe.wait_ge(ws_masked.h, ws_masked.at(layer, 1))
                for g in range(8):
                    if g == 0:
                        pe.wait_ge(v_ready.h, v_ready.at(layer, 4))
                    pe.wait_ge(dve_evac.h, dve_evac.at(layer, DVE_EVAC["V"] + 5 + g if g < 2 else DVE_EVAC["U"] + g - 1))
                    for tt in range(4):
                        mm = pe.matmul(psum[:, (4 + g % 2) * 512 + tt * P:(4 + g % 2) * 512 + (tt + 1) * P],
                                       vtok[:, tt * D + g * P:tt * D + (g + 1) * P], wsT[:, g * P:(g + 1) * P], start=True, stop=True)
                    mm.then_inc(mixed_ready.h, 1)
                    if g < 4:
                        f = (act_evac, ACT_EVAC["A"] + 7 + g // 2) if g % 2 == 0 else (dve_evac, DVE_EVAC["A"] + 7 + g // 2)
                    else:
                        f = (act_evac, ACT_EVAC["U"] + g - 3)
                    unit(0, UNIT["U"] + g, H, free=f)

                def branch(stage, body, operand, ready, prev=None):
                    i, k = body
                    for c in range(4):
                        if prev:
                            f = prev[c]
                        elif c % 2 == 0:
                            f = (act_evac, i * 2 + (ACT_EVAC[stage] + 2 * (k - 1) + c // 2 + 1))
                        else:
                            f = (dve_evac, i * 2 + (DVE_EVAC[stage] + 2 * (k - 1) + c // 2 + 1))
                        if c == 1:
                            pe.wait_ge(x_lo.h, x_lo.at(layer, ready))
                        unit(i, UNIT[stage] + 4 * k + c, H if c % 2 == 0 else operand, free=f)

                branch("BRA", (0, 0), opa, SPLIT["U"] + 8, [(act_evac, ACT_EVAC["U"] + 5 + c) for c in range(4)])
                with pe.Fori(0, 3) as i:
                    branch("BRA", (i, 1), opa, SPLIT["U"] + 8)

                for c in range(4):
                    f = (act_evac, ACT_EVAC["BRA"] + 7 + c // 2) if c % 2 == 0 else (dve_evac, DVE_EVAC["BRA"] + 7 + c // 2)
                    unit(0, UNIT["P"] + c, H, free=f)
                for c in range(4):
                    unit(0, UNIT["P"] + 4 + c, H, free=(act_evac, ACT_EVAC["P"] + c + 1))

                for q in range(2):
                    c = UNIT["POOL"] + q
                    unit_is_split(0, c)
                    for g in (2 * q, 2 * q + 1):
                        pe.wait_ge(x_lo.h, x_lo.at(layer, SPLIT["P"] + 2 * g + 2))
                        for nt in range(2):
                            k = 2 * g + nt
                            if k < 4:
                                pe.wait_ge(act_evac.h, act_evac.at(layer, ACT_EVAC["P"] + 5 + k))
                            elif k < 6:
                                pe.wait_ge(dve_evac.h, dve_evac.at(layer, DVE_EVAC["U"] + 3 + k))
                            elif k == 7:
                                pe.wait_ge(val_ready.h, val_ready.at(layer, SPLIT["POOL"] + 1))
                            for kt in range(2):
                                o = (c % RING) * UC + (g % 2) * 512 + kt * 256 + nt * P
                                hi, lo = tile(mid_hi, OPB[0] + 2 * g + kt), tile(mid_lo, OPB[1] + 2 * g + kt)
                                for m, (st, mv) in enumerate(passes(hi, lo, whi[:, o:o + P], wlo[:, o:o + P], False)):
                                    mm = pe.matmul(bank(k % 7), st, mv, start=(kt == 0 and m == 0), stop=(kt == 1 and m == 2))
                    mm.then_inc(unit_done.h, 1)

                branch("BRB", (0, 0), opb, SPLIT["POOL"] + 8, [(val_ready, SPLIT["POOL"] + n) for n in (3, 4, 8, 2)])
                branch("BRB", (0, 1), opb, SPLIT["POOL"] + 8)
                channel_sum(zsum_ready, zsum_ready.at(layer, 1))
                pe.wait_ge(ada_used.h, ada_used.at(layer, 4))
                ada_sum(layer, 0, ada_acc[:, :])
                branch("BRB", (0, 2), opb, SPLIT["POOL"] + 8)
                channel_sum(sq_added, sq_added.at(layer, SQ["C"] + 8))
                branch("BRB", (0, 3), opb, SPLIT["POOL"] + 8)

                for k in range(4):
                    pe.wait_ge(ada_used.h, ada_used.at(layer, 8 + 4 * k))
                    ada_sum(layer, 1 + k, ada_acc[:, :])
                    prev = None if k else [(act_evac, ACT_EVAC["BRB"] + 7), (dve_evac, DVE_EVAC["BRB"] + 7),
                                           (act_evac, ACT_EVAC["BRB"] + 8), (dve_evac, DVE_EVAC["BRB"] + 8)]
                    branch("BRC", (0, k), opa, SPLIT["C"] + 8, prev)

                for c in range(8):
                    if c % 4 == 0:
                        pe.wait_ge(ada_used.h, ada_used.at(layer, 24 + c))
                        ada_sum(layer, 5 + c // 4, ada_acc[:, :])
                    if c < 4:
                        f = (act_evac, ACT_EVAC["BRC"] + 7 + c // 2) if c % 2 == 0 else (dve_evac, DVE_EVAC["BRC"] + 7 + c // 2)
                    else:
                        f = (dve_evac, DVE_EVAC["OUT"] + c - 3)
                    unit(0, UNIT["OUT"] + c, opb, free=f, tiles=SPLIT["BRC"] if c == 0 else None)

                channel_sum(sq_added, sq_added.at(layer, SQ["OUT"] + 8))

                def ffn_units(i, m, k, prev=None):
                    for c in range(4):
                        if prev:
                            f = prev[c]
                        elif c % 2 == 0:
                            f = (act_evac, i * (2 * m) + (ACT_EVAC["FI"] + 2 * k - 1 + c // 2))
                        else:
                            f = (val_ready, i * (2 * m) + (SPLIT["FI"] + 2 * k - 1 + c // 2))
                        unit(i * m if m > 1 else i, UNIT["FI"] + 4 * k + c, H, free=f, tiles=SPLIT["N2"] if prev and c == 0 else None)

                prev = [(dve_evac, DVE_EVAC["OUT"] + 5 + c) for c in range(4)]
                pe.wait_ge(ada_used.h, ada_used.at(layer, 32))
                ada_sum(layer, 7, ada_acc[:, :])
                ffn_units(0, 1, 0, prev)
                ffn_units(0, 1, 1)
                with pe.Fori(0, 3) as i:
                    pe.wait_ge(ada_used.h, ada_used.at(layer, i * 4 + 36))
                    ada_sum(layer, i + 8, ada_acc[:, :])
                    ffn_units(i, 2, 2)
                    ffn_units(i, 2, 3)
                pe.wait_ge(ada_used.h, ada_used.at(layer, 48))
                ada_sum(layer, 11, ada_acc[:, :])
                with pe.Fori(0, 3) as i:
                    ffn_units(i, 1, 8)

                def ff_matmuls(kt, s, n, first, last):
                    w = slice(s * UC + n * P, s * UC + (n + 1) * P)
                    hi, lo = mid_hi[:, ds(kt * S, S)], mid_lo[:, ds(kt * S, S)]
                    for m, (st, mv) in enumerate(passes(hi, lo, whi[:, w], wlo[:, w], False)):
                        mm = pe.matmul(bank(n), st, mv, start=(first and m == 0), stop=(last and m == 2))
                    return mm

                def ff_unit(i, k, first=False):
                    c = UNIT["FO"] + k
                    unit_is_split(i, c)
                    pe.wait_ge(x_lo.h, x_lo.at(layer, i * 4 + (SPLIT["FI"] + k + 1)))
                    for n in range(8):
                        if first and n < 4:
                            order = (n - UNIT["FO"]) % 4
                            e = (act_evac, ACT_EVAC["FI"] + FT - 1 + order // 2) if order % 2 == 0 else (val_ready, SPLIT["FI"] + FT - 1 + order // 2)
                            pe.wait_ge(e[0].h, e[0].at(layer, e[1]))
                        if first and n == 4:
                            pe.wait_ge(ada_read.h, ada_read.at(layer, 12))
                        mm = ff_matmuls(i * 4 + k, c % RING, n, first, False)
                    mm.then_inc(unit_done.h, 1)

                ff_unit(0, 0, first=True)
                ff_unit(0, 1)
                with pe.Fori(0, 4) as i:
                    for k in range(4):
                        ff_unit(i, 2 + k)
                for k in range(4):
                    unit_is_split(0, UNITS - 4 + k)
                pe.wait_ge(x_lo.h, x_lo.at(layer, SPLIT["FI"] + FT))
                for n in range(8):
                    for k in range(4):
                        mm = ff_matmuls(FT - 4 + k, k, n, False, k == 3)
                        if n == 7:
                            mm.then_inc(unit_done.h, 1)
                    if n < 7:
                        mm.then_inc(ff_bank.h, 1)

            pe.wait_ge(sq_added.h, sq_added.at(DEPTH, 0))
            pe.matmul(bank(6), mean, ssum[:, :], start=True, stop=True).then_inc(stat_ready.h, 1)


def _tiles(w, n0, n):
    k = w.shape[0] // P
    return w[:, n0:n0 + n * P].reshape(k, P, n, P).transpose(2, 1, 0, 3).reshape(n, P, k * P)


def _pairs(a, b):
    return np.stack([a, b], axis=1).reshape(-1, P, UC)


def _columns(v):
    return v.reshape(-1, P).T


def kernel(x, c, w_ada, b_ada, g_mix, w_in, b_in, sgu_ln_g, sgu_ln_b, sgu_w_s, sgu_b_s, w_pa, pool_w, pool_scale,
           w_pb, conv_w, conv_b, conv_ln_g, conv_ln_b, w_pc, w_out, g_ffn, w_ffn_in, w_ffn_out, g_final):
    import concourse.bacc as bacc
    from concourse import mybir as _mybir
    from concourse.bass_utils import run_bass_kernel_spmd as run

    (x, c, w_ada, b_ada, g_mix, w_in, b_in, sgu_ln_g, sgu_ln_b, sgu_w_s, sgu_b_s, w_pa, pool_w, pool_scale,
     w_pb, conv_w, conv_b, conv_ln_g, conv_ln_b, w_pc, w_out, g_ffn, w_ffn_in, w_ffn_out, g_final) = (
        np.asarray(a) for a in (x, c, w_ada, b_ada, g_mix, w_in, b_in, sgu_ln_g, sgu_ln_b, sgu_w_s, sgu_b_s, w_pa,
                                pool_w, pool_scale, w_pb, conv_w, conv_b, conv_ln_g, conv_ln_b, w_pc, w_out, g_ffn,
                                w_ffn_in, w_ffn_out, g_final))

    stream = []
    for l in range(DEPTH):
        wi = w_in[l]
        for half in range(2):
            v = wi[:, BT["v"] * P + half * 512:BT["v"] * P + half * 512 + 512]
            stream.append(v.reshape(4, 2, P, 512).transpose(0, 2, 1, 3).reshape(4, P, UC))
        stream.append(_pairs(_tiles(wi, BT["ag"] * P, 8), _tiles(wi, BT["a"] * P, 8)))
        stream.append(_tiles(wi, BT["u"] * P, 8))
        stream.append(_pairs(_tiles(wi, BT["gate"] * P, 8), _tiles(w_pa[l], 0, 8)))
        stream.append(_tiles(wi, BT["p"] * P, 8))
        stream.append(pool_w[l].reshape(2, 2, 2, P, 256).transpose(0, 3, 1, 2, 4).reshape(2, P, UC))
        stream.append(_pairs(_tiles(wi, (BT["gate"] + 8) * P, 8), _tiles(w_pb[l], 0, 8)))
        stream.append(_pairs(_tiles(wi, (BT["gate"] + 16) * P, 8), _tiles(w_pc[l], 0, 8)))
        stream.append(_tiles(w_out[l], 0, 8))
        stream.append(_pairs(_tiles(w_ffn_in[l], 0, FT), _tiles(w_ffn_in[l], D_FF, FT)))
        stream.append(w_ffn_out[l].reshape(FT, P, D))
    weights = np.concatenate(stream)

    a = w_ada.reshape(DEPTH, 4, 2, P, 6, 2, 512).transpose(0, 4, 5, 1, 3, 2, 6).reshape(DEPTH, 6, 8, P, UC)
    b = b_ada.reshape(DEPTH, 6, D)
    order = [(0, 0), (0, 1)]
    for l in range(DEPTH):
        order += [(l, j) for j in range(2, 6)] + [((l + 1) % DEPTH, j) for j in (0, 1)]
    ada_stream = np.concatenate([a[l, j] for l, j in order])
    b_cols = np.concatenate([_columns(b[l, j]) for l, j in order], axis=1)

    cols = np.stack([np.concatenate([
        _columns(g_mix[l]), _columns(b_in[l]), _columns(g_ffn[l]), _columns(conv_b[l]), _columns(conv_ln_g[l]),
        _columns(conv_ln_b[l]), _columns(pool_scale[l]),
        conv_w[l].reshape(TAPS, CT, P).transpose(2, 1, 0).reshape(P, CT * TAPS)], axis=1) for l in range(DEPTH)])
    rows = np.concatenate([np.stack([b_in[l][BT["v"] * P:BT["v"] * P + D], sgu_ln_g[l], sgu_ln_b[l],
                                     sgu_b_s[l].reshape(-1)]) for l in range(DEPTH)])
    ws = sgu_w_s.transpose(0, 3, 1, 2).reshape(DEPTH, P, 8 * P)
    head = np.array([[win / min(t + 1, win) for t in range(WMAX)] for win in WINDOWS], np.float32).reshape(1, -1)
    f = np.float32
    fixed = np.concatenate([b_cols, _columns(g_final), _columns(c), np.full((P, 1), EPS, f), np.repeat(head, P, 0),
                            np.eye(P, dtype=f), np.ones((P, P), f), np.full((P, P), 1.0 / D, f)], axis=1)
    xT = x[0].reshape(S, CT, P).transpose(2, 1, 0).reshape(P, CT * S)

    nc = bacc.Bacc("TRN2", target_bir_lowering=False, num_devices=1, dynamic_dma_scratch_size=1024)
    arrays, args = {}, []
    for name, arr in (("xT", xT), ("fixed", fixed), ("cols", cols), ("rows", rows), ("ws", ws), ("w_ada", ada_stream),
                      ("weights", weights)):
        arrays[name + "_in"] = np.ascontiguousarray(arr)
        args.append(nc.dram_tensor(name + "_in", arr.shape, _mybir.dt.float32, kind="ExternalInput").ap())
    args.append(nc.dram_tensor("y_out", (P, CT * S), _mybir.dt.float32, kind="ExternalOutput").ap())
    trunk(nc, *args)
    r = run(nc, [arrays], core_ids=[0])
    y = r.results[0]["y_out"]
    return np.ascontiguousarray(y.reshape(P, CT, S).transpose(2, 1, 0).reshape(1, S, D))
```

```python
import concourse.bass as bass
from concourse import mybir
import numpy as np
from contextlib import ExitStack

P = 128
D = 1024
S = 512
HS = S // 2
DEPTH = 2
CT = D // P
D_FF = 2816
FT = D_FF // P
TAPS = 31
PAD = TAPS - 1
WINDOWS = (2, 4, 8, 16)
WMAX = max(WINDOWS)
EPS = 1e-6

UC = 1024
UNIT, at = {}, 0
for stage, n in (("V", 8), ("A", 16), ("U", 8), ("BRA", 16), ("P", 8), ("POOL", 2), ("BRB", 16),
                 ("BRC", 16), ("OUT", 8), ("FI", 2 * FT), ("FO", FT)):
    UNIT[stage] = at
    at += n
UNITS = at
RING = 4
RAW = 2

def bases(*counts):
    out, n = {}, 0
    for name, k in counts:
        out[name] = n
        n += k
    return out, n


ACT_EVAC, N_ACT_EVAC = bases(("A", 8), ("U", 8), ("BRA", 8), ("P", 8), ("BRB", 8), ("BRC", 8), ("FI", FT))
DVE_EVAC, N_DVE_EVAC = bases(("V", 8), ("A", 8), ("U", 8), ("BRA", 8), ("BRB", 8), ("BRC", 8), ("OUT", 12), ("FO", 16))
SPLIT, N_SPLIT = bases(("N1", 16), ("U", 8), ("P", 8), ("POOL", 8), ("C", 8), ("BRC", 8), ("N2", 16), ("FI", FT))
SQ, N_SQ = bases(("C", 8), ("OUT", 12), ("FO", 16))
FO_B = (6, 0, 1, 2, 3, 4, 5, 7)
ADA_HALVES = 12
ADA_CHUNKS = 4 * ADA_HALVES

A_TAPS = (0, 12, 20, 28, 36, 44, 57, 70, 74)
U_TAPS = A_TAPS[-1]
BRA_TAPS = (114, 127, 140, 153, 166, 179, 192, 205, 210)
BRB_TAPS = (210, 220, 230, 239, 8 * TAPS)
DVE_STEPS = 382

COL, N_COL = bases(("g_mix", 8), ("b_in", 64), ("g_ffn", 8), ("conv_b", 8), ("conv_g", 8), ("conv_lb", 8),
                   ("pool_scale", 8), ("conv_w", 8 * TAPS))
FIX, N_FIX = bases(("b_ada", 48 * DEPTH + 16), ("g_final", 8), ("c", 8), ("eps", 1), ("head", 4 * WMAX),
                   ("ident", P), ("ones", P), ("mean", P))
BT = {"u": 0, "v": 8, "p": 16, "a": 24, "ag": 32, "gate": 40}
GT_M, SH_F, SC_F, GT_F, SH_M, SC_M = (8 * j for j in range(6))


class Sem:

    def __init__(self, handle, per_layer=0, start=0, unit=1):
        self.h, self.per, self.start, self.unit = handle, per_layer, start, unit

    def at(self, layer, n):
        assert not isinstance(n, int) or n + self.start > 0
        return (layer * self.per + (n + self.start)) * self.unit


class Steps:

    def __init__(self, eng, sem):
        self.eng, self.sem, self.layer, self.n, self.loop = eng, sem, 0, 0, None

    def did(self, ins):
        ins.then_inc(self.sem.h, 1)
        self.n += 1

    def settle(self):
        n = self.n if self.loop is None else self.loop + self.n
        self.eng.wait_ge(self.sem.h, self.sem.at(self.layer, n))


def trunk(nc, xT, fixed, cols, rows, ws, w_ada, weights, out):
    f32, f32r = mybir.dt.float32, mybir.dt.float32r
    ALU, ACT = mybir.AluOpType, mybir.ActivationFunctionType
    AX = mybir.AxisListType
    ds = bass.ds

    top = [1152]

    def aligned(n):
        return -(-n // 32) * 32

    def place(name, width, dt=f32, offset=None):
        if offset is None:
            offset = top[0]
            top[0] += aligned(4 * width)
        return nc.alloc_sbuf_tensor_at(name, [P, width], dt, offset=offset), offset

    x, _ = place("x", CT * S)
    raw, _ = place("raw", RAW * UC)
    whi, _ = place("whi", RING * UC, f32r)
    wlo, _ = place("wlo", RING * UC, f32r)
    h_hi, h_at = place("h_hi", CT * S, f32r)
    h_lo, _ = place("h_lo", CT * S, f32r)
    mid_lo, lo_at = place("mid_lo", FT * S, f32r)
    mid_hi, hi_at = place("mid_hi", FT * S, f32r)
    merged, merged_at = place("merged", CT * S)
    ada_raw, _ = place("ada_raw", 2 * UC)
    ada_acc, _ = place("ada_acc", 512)
    atmp, _ = place("atmp", 2 * S)
    dtmp, _ = place("dtmp", 2 * S)
    sq, _ = place("sq", 2 * S)
    ssum, _ = place("ssum", S)
    rstd, _ = place("rstd", S)
    col, _ = place("col", N_COL)
    fix, _ = place("fix", N_FIX)
    ada, _ = place("ada", 48)
    gain, _ = place("gain", CT)
    cact, _ = place("cact", CT)
    vbn, _ = place("vbn", 4 * 2 * 6)
    vmv, _ = place("vmv", 4 * 2)
    vstd, _ = place("vstd", 4)
    FREE = FT - 2 * CT
    OPA, OPB = (FREE, 0), (FREE + CT, CT)
    gap = lo_at + 4 * 2 * CT * S
    assert gap + 4 * 2 * FREE * S == hi_at + 4 * FREE * S
    ZW = PAD + S
    ws_at = gap + aligned(4 * CT * ZW)
    pro_at = ws_at + 4 * 8 * P
    assert pro_at <= gap + 4 * 2 * FREE * S
    zc, _ = place("zc", CT * ZW, offset=gap)
    wsT, _ = place("wsT", 8 * P, offset=ws_at)
    vtok, _ = place("vtok", 4 * D, offset=lo_at + 4 * CT * S)
    PW = WMAX - 1 + S
    ptmp, _ = place("ptmp", 2 * PW, offset=lo_at)
    wsum, _ = place("wsum", 2 * PW, offset=lo_at + aligned(4 * 2 * PW))
    bc, _ = place("bc", 4 * D, offset=merged_at)
    pro_raw = [place(f"pro_raw{h}", 4 * UC, offset=lo_at + 4 * 4 * UC * h if h < 3 else pro_at)[0]
               for h in range(4)]
    pro_acc, _ = place("pro_acc", 4 * 512, offset=h_at)
    psum = nc.alloc_psum_tensor("psum", [P, 8 * 512], f32)

    def bank(b):
        return psum[:, 512 * b:512 * b + 512]

    def tile(t, k, w=S):
        return t[:, k * w:(k + 1) * w]

    def half(t, k, f, w=S):
        return t[:, k * w + f * HS:k * w + (f + 1) * HS]

    def half3(t, k0, k1, f):
        return t[:, :].rearrange("p (k t) -> p k t", k=CT)[:, k0:k1, f * HS:(f + 1) * HS]

    def c1(t, k):
        return t[:, k:k + 1]

    ident = fix[:, FIX["ident"]:FIX["ident"] + P]
    ones = fix[:, FIX["ones"]:FIX["ones"] + P]
    mean = fix[:, FIX["mean"]:FIX["mean"] + P]
    eps = c1(fix, FIX["eps"])

    ctx = ExitStack()
    with ctx:
        def sem(name, per_layer=0, start=0, unit=1):
            return Sem(ctx.enter_context(nc.semaphore(name)), per_layer, start, unit)

        fix_in, x_in = sem("fix_in"), sem("x_in")
        pro_in = [sem(f"pro_in{h}") for h in range(7)]
        raw_in = [sem(f"raw_in{s}", UNITS // RAW, unit=16) for s in range(RAW)]
        ada_in = [sem(f"ada_in{s}", ADA_CHUNKS // 2, unit=16) for s in range(2)]
        col_in = sem("col_in", 1, unit=16)
        layer_in = sem("layer_in", 5, unit=16)
        out_done = sem("out_done")
        w_hi_done = sem("w_hi_done", UNITS)
        act_evac = sem("act_evac", N_ACT_EVAC)
        x_hi = sem("x_hi", N_SPLIT)
        sq_ready = sem("sq_ready", N_SQ, 8)
        std_ready = sem("std_ready", 6, 2)
        v_gelu = sem("v_gelu", 8)
        silu_ready = sem("silu_ready", 8)
        c_ready = sem("c_ready")
        w_lo_done = sem("w_lo_done", UNITS, RAW)
        ws_masked = sem("ws_masked", 1)
        unit_done = sem("unit_done", UNITS, RING)
        mixed_ready = sem("mixed_ready", 8)
        stat_ready = sem("stat_ready", 6, 2)
        ada_ready = sem("ada_ready", ADA_HALVES, 4)
        ff_bank = sem("ff_bank", 15)
        out_half = sem("out_half", 4)
        dve_evac = sem("dve_evac", N_DVE_EVAC)
        val_ready = sem("val_ready", N_SPLIT)
        x_lo = sem("x_lo", N_SPLIT)
        sq_added = sem("sq_added", N_SQ, 8 + 2)
        zsum_ready = sem("zsum_ready", 1)
        centered = sem("centered", 8)
        vstat_ready = sem("vstat_ready", 4)
        v_ready = sem("v_ready", 4)
        added = sem("added", 8)
        ada_used = sem("ada_used", ADA_CHUNKS, 2)
        ada_read = sem("ada_read", ADA_HALVES, 4)
        pro_acc_ready = sem("pro_acc_ready")
        dve_step = sem("dve_step", DVE_STEPS)
        last_std = sem("last_std")
        y_ready = sem("y_ready")

        block = ctx.enter_context(nc.Block())

        @block.sync
        def _(sp):
            sp.dma_start(fix[:, :], fixed[:, :]).then_inc(fix_in.h, 16)
            sp.dma_start(x[:, :], xT[:, :]).then_inc(x_in.h, 16)
            for h in range(3):
                sp.dma_start(pro_raw[h][:, :].rearrange("p (c n) -> p c n", c=4),
                             w_ada[4 * h:4 * h + 4, :, :].rearrange("c p n -> p c n")).then_inc(pro_in[h].h, 16)
            for c in range(4):
                if c == 2:
                    for u in range(RAW):
                        sp.dma_start(tile(raw, u, UC), weights[u, :, :]).then_inc(raw_in[u].h, 16)
                sp.dma_start(tile(pro_raw[3], c, UC), w_ada[12 + c, :, :]).then_inc(pro_in[3 + c].h, 16)

            with sp.Fori(0, DEPTH) as layer:
                sp.dma_start(col[:, :], cols[ds(layer, 1), :, :].rearrange("a p n -> p (a n)")).then_inc(col_in.h, 16)

                def load_unit(i, c):
                    sp.wait_ge(w_lo_done.h, w_lo_done.at(layer, i * 4 + (c - RAW + 1)))
                    sp.dma_start(tile(raw, c % RAW, UC), weights[ds(layer * UNITS + (i * 4 + c), 1), :, :]
                                 .rearrange("a p n -> p (a n)")).then_inc(raw_in[c % RAW].h, 16)

                def load_ada(c):
                    i, k, m = c
                    sp.wait_ge(ada_used.h, ada_used.at(layer, i * m + (k - 1)))
                    sp.dma_start(tile(ada_raw, k % 2, UC), w_ada[ds(layer * ADA_CHUNKS + (i * m + (k + 16)), 1), :, :]
                                 .rearrange("a p n -> p (a n)")).then_inc(ada_in[k % 2].h, 16)

                for c in (2, 3):
                    load_unit(0, c)
                for r in range(4):
                    sp.dma_start(tile(bc, r, D), rows[ds(layer * 4 + r, 1), :].to_broadcast([P, D])).then_inc(layer_in.h, 16)
                sp.dma_start(wsT[:, :], ws[ds(layer, 1), :, :].rearrange("a p n -> p (a n)")).then_inc(layer_in.h, 16)
                with sp.Fori(0, 14) as i:
                    for c in range(4):
                        load_unit(i, 4 + c)
                with sp.Fori(0, 4) as i:
                    for c in range(4):
                        if c % 2 == 0:
                            load_ada((i, c // 2, 2))
                        load_unit(i, 60 + c)
                for c in (76, 77):
                    load_unit(0, c)
                with sp.Fori(0, 4) as i:
                    for c in range(4):
                        load_ada((i, 8 + c, 4))
                        load_unit(i, 78 + c)
                for c, chunks in ((94, (24,)), (95, (25, 26)), (96, (27,)), (97, (28, 29)), (98, (30, 31)), (99, ()),
                                  (100, ()), (101, ())):
                    for k in chunks:
                        load_ada((0, k, 4))
                    load_unit(0, c)
                with sp.Fori(0, 8) as i:
                    for c in range(4):
                        if c % 2 == 0:
                            load_ada((i, 32 + c // 2, 2))
                        load_unit(i, 102 + c)
                with sp.Fori(0, 8) as i:
                    for c in range(4):
                        load_unit(i, 134 + c)

            for e in range(4):
                f, k = e // 2, e % 2 * 4
                sp.wait_ge(y_ready.h, 4 * e + 4)
                sp.dma_start(half3(out, k, k + 4, f), half3(x, k, k + 4, f)).then_inc(out_done.h, 16)
            sp.wait_ge(out_done.h, 16 * 4)

        @block.gpsimd
        def _(pool):
            pool.sem_inc(w_lo_done.h, RAW)

            def low_part(i, c, layer):
                s = c % RING
                pool.wait_ge(w_hi_done.h, w_hi_done.at(layer, i * 4 + (c + 1)))
                pool.tensor_tensor(tile(wlo, s, UC), tile(raw, c % RAW, UC), tile(whi, s, UC).bitcast(f32),
                                   ALU.subtract).then_inc(w_lo_done.h, 1)

            for c in range(2):
                low_part(0, c, 0)
            with pool.Fori(0, DEPTH) as layer:
                for c in range(2, 9):
                    low_part(0, c, layer)
                pool.wait_ge(layer_in.h, layer_in.at(layer, 5))
                low_part(0, 9, layer)
                w3 = wsT[:, :].rearrange("p (g t) -> p g t", g=8)
                pool.affine_select(out=w3, in_=w3, compare_op=ALU.is_ge, fill=0.0, base=0,
                                   pattern=[[0, 8], [1, P]], channel_multiplier=-1).then_inc(ws_masked.h, 1)
                with pool.Fori(0, (UNITS - 8) // 4) as i:
                    for c in range(4):
                        low_part(i, 10 + c, layer)

        @block.scalar
        def _(act):
            A = nc.scalar.activation

            act.wait_ge(fix_in.h, 16)
            A(cact[:, :], fix[:, FIX["c"]:FIX["c"] + CT], ACT.Silu).then_inc(c_ready.h, 1)
            act.wait_ge(x_in.h, 16)
            for k in range(CT):
                if k >= 2:
                    act.wait_ge(sq_added.h, k + 1)
                A(tile(sq, k % 2), tile(x, k), ACT.Square).then_inc(sq_ready.h, 1)

            def std(layer, n_stat, f):
                act.wait_ge(stat_ready.h, stat_ready.at(layer, n_stat))
                A(half(rstd, 0, f), half(bank(6), 0, f), ACT.Sqrt, bias=eps).then_inc(std_ready.h, 1)

            def weight_hi(i, c, layer):
                act.wait_ge(raw_in[c % RAW].h, raw_in[c % RAW].at(layer, i * 2 + (c // 2 + 1)))
                act.wait_ge(unit_done.h, unit_done.at(layer, i * 4 + (c - RING + 1)))
                nc.scalar.copy(tile(whi, c % RING, UC), tile(raw, c % RAW, UC)).then_inc(w_hi_done.h, 1)

            std(0, -1, 0)
            std(0, 0, 1)
            weight_hi(0, 0, 0)
            weight_hi(0, 1, 0)

            with act.Fori(0, DEPTH) as layer:

                def unit_is_done(i, c):
                    act.wait_ge(unit_done.h, unit_done.at(layer, i * 4 + (c + 1)))

                def split_hi(hi, t, stage, k):
                    act.wait_ge(val_ready.h, val_ready.at(layer, SPLIT[stage] + k + 1))
                    nc.scalar.copy(tile(hi, t), tile(dtmp, k % 2)).then_inc(x_hi.h, 1)

                def norm_half(f, shift, stage):
                    for k in range(CT):
                        e = f * CT + k
                        act.wait_ge(val_ready.h, val_ready.at(layer, SPLIT[stage] + e + 1))
                        A(half(h_hi, k, f), tile(dtmp, e % 4, HS), ACT.Identity, bias=c1(ada, shift + k)).then_inc(x_hi.h, 1)

                def square(src, stage, e, f=None):
                    act.wait_ge(sq_added.h, sq_added.at(layer, SQ[stage] + e - 1))
                    A(tile(sq, e % 2) if f is None else half(sq, e % 2, f), src, ACT.Square).then_inc(sq_ready.h, 1)

                act.wait_ge(col_in.h, col_in.at(layer, 1))
                norm_half(0, SH_M, "N1")
                weight_hi(0, 2, layer)
                weight_hi(0, 3, layer)
                norm_half(1, SH_M, "N1")

                act.wait_ge(layer_in.h, layer_in.at(layer, 5))
                for u in range(8):
                    weight_hi(0, u + 4, layer)
                    if u % 4 == 3:
                        for tt in range(4):
                            n = u // 4 * 4 + tt
                            v = vtok[:, tt * D + u // 4 * 512:tt * D + u // 4 * 512 + 512]
                            act.wait_ge(dve_evac.h, dve_evac.at(layer, DVE_EVAC["V"] + n + 1))
                            A(v, v, ACT.Gelu).then_inc(v_gelu.h, 1)

                for p in range(8):
                    u = UNIT["A"] + 2 * p
                    unit_is_done(0, u)
                    if p >= 2:
                        act.wait_ge(dve_evac.h, dve_evac.at(layer, DVE_EVAC["A"] + p - 1))
                    A(tile(atmp, p % 2), bank(u % 4), ACT.Sigmoid, bias=c1(col, COL["b_in"] + BT["ag"] + p)).then_inc(act_evac.h, 1)
                    weight_hi(0, u + 4, layer)
                    weight_hi(0, u + 5, layer)
                    if p == 0:
                        act.wait_ge(vstat_ready.h, vstat_ready.at(layer, 4))
                        A(vstd[:, :].rearrange("p (t a) -> p t a", a=1), vmv[:, :].rearrange("p (t a) -> p t a", a=2)[:, :, 1:2], ACT.Sqrt, bias=eps).then_inc(std_ready.h, 1)

                for g in range(8):
                    u = UNIT["U"] + g
                    unit_is_done(0, u)
                    if g < 2:
                        act.wait_ge(dve_evac.h, dve_evac.at(layer, DVE_EVAC["A"] + 7 + g))
                    else:
                        act.wait_ge(val_ready.h, val_ready.at(layer, SPLIT["U"] + g - 1))
                    A(tile(atmp, g % 2), bank(u % 4), ACT.Gelu, bias=c1(col, COL["b_in"] + BT["u"] + g)).then_inc(act_evac.h, 1)
                    weight_hi(0, u + 4, layer)
                    split_hi(mid_hi, OPA[0] + g, "U", g)

                def gate(branch, stage, n):
                    A(tile(atmp, n % 2), bank((UNIT[stage] + 2 * n) % 4), ACT.Sigmoid,
                      bias=c1(col, COL["b_in"] + BT["gate"] + 8 * branch + n)).then_inc(act_evac.h, 1)

                for n in range(8):
                    u = UNIT["BRA"] + 2 * n
                    unit_is_done(0, u)
                    if n < 2:
                        act.wait_ge(val_ready.h, val_ready.at(layer, SPLIT["U"] + 7 + n))
                    else:
                        act.wait_ge(dve_evac.h, dve_evac.at(layer, DVE_EVAC["BRA"] + n - 1))
                    gate(0, "BRA", n)
                    weight_hi(0, u + 4, layer)
                    weight_hi(0, u + 5, layer)

                for k in range(8):
                    u = UNIT["P"] + k
                    unit_is_done(0, u)
                    if k >= 2:
                        act.wait_ge(val_ready.h, val_ready.at(layer, SPLIT["P"] + k - 1))
                    A(ptmp[:, k % 2 * PW + WMAX - 1:(k % 2 + 1) * PW], bank(u % 4), ACT.Identity,
                      bias=c1(col, COL["b_in"] + BT["p"] + k)).then_inc(act_evac.h, 1)
                    weight_hi(0, u + 4, layer)
                    split_hi(mid_hi, OPB[0] + k, "P", k)

                for q in range(2):
                    if q == 0:
                        weight_hi(0, UNIT["POOL"] + 4, layer)
                    for k in range(4 * q, 4 * q + 4):
                        split_hi(mid_hi, OPB[0] + k, "POOL", k)
                weight_hi(0, UNIT["POOL"] + 5, layer)

                for n in range(8):
                    u = UNIT["BRB"] + 2 * n
                    if n == 6:
                        act.wait_ge(stat_ready.h, stat_ready.at(layer, 2))
                        A(rstd[:, :], bank(6), ACT.Sqrt, bias=eps).then_inc(std_ready.h, 1)
                        weight_hi(0, u + 4, layer)
                        for k in range(CT):
                            act.wait_ge(val_ready.h, val_ready.at(layer, SPLIT["C"] + k + 1))
                            if k >= 2:
                                act.wait_ge(x_lo.h, x_lo.at(layer, SPLIT["C"] + k - 1))
                            A(tile(sq, k % 2), tile(dtmp, k % 2), ACT.Silu, bias=c1(col, COL["conv_lb"] + k)).then_inc(silu_ready.h, 1)
                            act.wait_ge(silu_ready.h, silu_ready.at(layer, k + 1))
                            nc.scalar.copy(tile(mid_hi, OPA[0] + k), tile(sq, k % 2)).then_inc(x_hi.h, 1)
                    unit_is_done(0, u)
                    if n < 2:
                        act.wait_ge(dve_evac.h, dve_evac.at(layer, DVE_EVAC["BRA"] + 7 + n))
                    else:
                        act.wait_ge(added.h, added.at(layer, n - 1))
                    gate(1, "BRB", n)
                    if n != 6:
                        weight_hi(0, u + 4, layer)
                    weight_hi(0, u + 5, layer)
                    if n == 4:
                        for k in range(CT):
                            act.wait_ge(centered.h, centered.at(layer, k + 1))
                            square(zc[:, k * ZW + PAD:(k + 1) * ZW], "C", k)

                for n in range(8):
                    u = UNIT["BRC"] + 2 * n
                    unit_is_done(0, u)
                    if n < 2:
                        act.wait_ge(added.h, added.at(layer, 7 + n))
                    else:
                        act.wait_ge(val_ready.h, val_ready.at(layer, SPLIT["BRC"] + n - 1))
                    gate(2, "BRC", n)
                    weight_hi(0, u + 4, layer)
                    split_hi(mid_hi, OPB[0] + n, "BRC", n)
                    weight_hi(0, u + 5, layer)

                for n in range(4):
                    weight_hi(0, UNIT["OUT"] + n + 4, layer)
                    act.wait_ge(dve_evac.h, dve_evac.at(layer, DVE_EVAC["OUT"] + n + 1))
                    square(tile(x, n), "OUT", n)

                def square_half(stage, e, n, f):
                    act.wait_ge(dve_evac.h, dve_evac.at(layer, DVE_EVAC[stage] + e + 1))
                    square(half(x, n, f), stage, e, f)

                for n in range(4, 8):
                    square_half("OUT", n, n, 0)
                std(layer, 3, 0)
                for k in range(CT):
                    e = k
                    act.wait_ge(val_ready.h, val_ready.at(layer, SPLIT["N2"] + e + 1))
                    A(half(h_hi, k, 0), tile(dtmp, e % 4, HS), ACT.Identity, bias=c1(ada, SH_F + k)).then_inc(x_hi.h, 1)
                    if k % 2:
                        weight_hi(0, UNIT["OUT"] + 8 + k // 2, layer)
                        square_half("OUT", 8 + k // 2, 4 + k // 2, 1)
                std(layer, 4, 1)
                norm_half(1, SH_F, "N2")

                with act.Fori(0, FT // 2) as i:
                    for k in range(2):
                        c = UNIT["FI"] + 2 * k
                        unit_is_done(i, c)
                        act.wait_ge(val_ready.h, val_ready.at(layer, i * 2 + (SPLIT["FI"] + k - 1)))
                        A(tile(atmp, k), bank(c % 4), ACT.Silu).then_inc(act_evac.h, 1)
                        weight_hi(i, c + 4, layer)
                        act.wait_ge(val_ready.h, val_ready.at(layer, i * 2 + (SPLIT["FI"] + k + 1)))
                        nc.scalar.copy(mid_hi[:, ds((i * 2 + k) * S, S)], tile(dtmp, k)).then_inc(x_hi.h, 1)
                        weight_hi(i, c + 5, layer)

                for c in range(146, 148):
                    weight_hi(0, c, layer)
                with act.Fori(0, 4) as i:
                    for c in range(4):
                        weight_hi(i, 148 + c, layer)
                for e in range(8):
                    square_half("FO", e, e, 0)
                std(layer, 5, 0)
                for e, n in enumerate(FO_B):
                    square_half("FO", 8 + e, n, 1)
                    if e == 0:
                        weight_hi(0, UNITS, layer)
                        weight_hi(0, UNITS + 1, layer)
                std(layer, 6, 1)

        @block.vector
        def _(dve):
            V = nc.vector
            steps = Steps(dve, dve_step)

            def did(ins):
                steps.did(ins)

            def then(ins):
                steps.did(ins)
                steps.settle()

            def add_square(layer, stage, e, f=None, first=False):
                n = e - CT if stage is None else SQ[stage] + e
                dve.wait_ge(sq_ready.h, sq_ready.at(layer, n + 1))
                total, square = (ssum[:, :], tile(sq, e % 2)) if f is None else (half(ssum, 0, f), half(sq, e % 2, f))
                if first:
                    V.tensor_copy(total, square).then_inc(sq_added.h, 1)
                else:
                    dve.wait_ge(sq_added.h, sq_added.at(layer, n))
                    V.tensor_tensor(total, total, square, ALU.add).then_inc(sq_added.h, 1)

            def ada_finish(scratch, layer, n, at_col, bias_at, settle=True):
                dve.wait_ge(ada_ready.h, ada_ready.at(layer, n + 1))
                r3 = scratch.rearrange("p (c n) -> p c n", c=4)
                V.tensor_tensor(r3, bank(4).rearrange("p (c n) -> p c n", c=4),
                                ident.rearrange("p (a n) -> p a n", a=1).to_broadcast([P, 4, P]), ALU.mult).then_inc(ada_read.h, 1)
                dve.wait_ge(ada_read.h, ada_read.at(layer, n + 1))
                then(V.reduce_sum(ada[:, ds(at_col, 4)], r3, AX.X))
                did(V.tensor_tensor(ada[:, ds(at_col, 4)], ada[:, ds(at_col, 4)], fix[:, ds(bias_at, 4)], ALU.add))
                if settle:
                    steps.settle()

            dve.wait_ge(fix_in.h, 16)
            dve.sem_inc(sq_added.h, 2)
            dve.sem_inc(ada_used.h, 2)
            dve.wait_ge(c_ready.h, 1)
            for k in range(CT):
                add_square(0, None, k, first=k == 0)
            for h in range(4):
                acc = tile(pro_acc, h)
                for k in range(CT):
                    if h == 3 and k % 2 == 0:
                        dve.wait_ge(pro_in[3 + k // 2].h, 16)
                    elif k == 0:
                        dve.wait_ge(pro_in[h].h, 16)
                    w = tile(pro_raw[h], k)
                    if k == 0:
                        then(V.tensor_scalar(acc, w, c1(cact, k), None, ALU.mult))
                    elif k < CT - 1:
                        then(V.scalar_tensor_tensor(out=acc, in0=w, scalar=c1(cact, k), in1=acc, op0=ALU.mult, op1=ALU.add))
                    else:
                        V.scalar_tensor_tensor(out=acc, in0=w, scalar=c1(cact, k), in1=acc,
                                               op0=ALU.mult, op1=ALU.add).then_inc(pro_acc_ready.h, 1)
                if h:
                    ada_finish(tile(atmp, 0), 0, h - 1 - 4, SH_M + 4 * (h - 1), FIX["b_ada"] + 4 * (h - 1))
            dve.wait_ge(std_ready.h, std_ready.at(0, -1))
            then(V.reciprocal(half(rstd, 0, 0), half(rstd, 0, 0)))
            ada_finish(tile(atmp, 0), 0, -1, SH_M + 12, FIX["b_ada"] + 12)
            dve_step.start = steps.n
            steps.n = 0

            with dve.Fori(0, DEPTH) as layer:
                steps.layer = layer

                def unit_is_done(i, c):
                    dve.wait_ge(unit_done.h, unit_done.at(layer, i * 4 + (c + 1)))

                def split_lo(val, hi, lo, stage, k):
                    dve.wait_ge(x_hi.h, x_hi.at(layer, SPLIT[stage] + k + 1))
                    V.tensor_tensor(lo, val, hi.bitcast(f32), ALU.subtract).then_inc(x_lo.h, 1)

                def slot_is_split(stage, k):
                    if SPLIT[stage] + k >= 2:
                        dve.wait_ge(x_lo.h, x_lo.at(layer, SPLIT[stage] + k - 1))

                def ada_chunk(i, k, m):
                    dve.wait_ge(ada_in[k % 2].h, ada_in[k % 2].at(layer, i * (m // 2) + (k // 2 + 1)))
                    w0, w1 = (ada_raw[:, k % 2 * UC + 512 * j:k % 2 * UC + 512 * (j + 1)] for j in range(2))
                    kt = 2 * (k % 4)
                    if k % 4 == 0:
                        then(V.tensor_scalar(ada_acc[:, :], w0, c1(cact, kt), None, ALU.mult))
                    else:
                        dve.wait_ge(ada_used.h, ada_used.at(layer, i * m + k))
                        then(V.scalar_tensor_tensor(out=ada_acc[:, :], in0=w0, scalar=c1(cact, kt), in1=ada_acc[:, :],
                                                    op0=ALU.mult, op1=ALU.add))
                    V.scalar_tensor_tensor(out=ada_acc[:, :], in0=w1, scalar=c1(cact, kt + 1), in1=ada_acc[:, :],
                                           op0=ALU.mult, op1=ALU.add).then_inc(ada_used.h, 1)

                def finish(n, settle=True):
                    ada_finish(rstd[:, :], layer, n, 4 * n, layer * 48 + (FIX["b_ada"] + 16 + 4 * n), settle)

                def gains(g, scale):
                    then(V.tensor_scalar(gain[:, :], ada[:, scale:scale + CT], 1.0, None, ALU.add))
                    then(V.tensor_tensor(gain[:, :], gain[:, :], g, ALU.mult))

                def norm_half(f, shift, stage, between=None):
                    for k in range(CT + 2):
                        if k < CT:
                            e = SPLIT[stage] + f * CT + k
                            if e >= 4:
                                dve.wait_ge(x_lo.h, x_lo.at(layer, e - 3))
                            V.scalar_tensor_tensor(out=tile(dtmp, k % 4, HS), in0=half(x, k, f), scalar=c1(gain, k),
                                                   in1=half(rstd, 0, f), op0=ALU.mult, op1=ALU.mult).then_inc(val_ready.h, 1)
                        if k >= 2:
                            dve.wait_ge(x_hi.h, x_hi.at(layer, SPLIT[stage] + f * CT + k - 1))
                            V.scalar_tensor_tensor(out=half(h_lo, k - 2, f), in0=tile(dtmp, (k - 2) % 4, HS),
                                                   scalar=c1(ada, shift + k - 2), in1=half(h_hi, k - 2, f).bitcast(f32),
                                                   op0=ALU.add, op1=ALU.subtract).then_inc(x_lo.h, 1)
                        if between and k < CT:
                            between(k)

                def half_reciprocal(layer_, n_std, f):
                    dve.wait_ge(std_ready.h, std_ready.at(layer_, n_std))
                    then(V.reciprocal(half(rstd, 0, f), half(rstd, 0, f)))

                def half_update(psum_half, n, f, gate):
                    V.scalar_tensor_tensor(out=half(x, n, f), in0=psum_half, scalar=c1(ada, gate + n), in1=half(x, n, f),
                                           op0=ALU.mult, op1=ALU.add).then_inc(dve_evac.h, 1)

                def conv_taps(first, last):
                    for n in range(first, last):
                        j, k = divmod(n, TAPS)
                        z = zc[:, j * ZW + k:j * ZW + k + S]
                        w = c1(col, COL["conv_w"] + j * TAPS + k)
                        if k == 0:
                            then(V.tensor_scalar(bank(7), z, w, c1(col, COL["conv_b"] + j), ALU.mult, ALU.add))
                        elif k < TAPS - 1:
                            then(V.scalar_tensor_tensor(out=bank(7), in0=z, scalar=w, in1=bank(7), op0=ALU.mult, op1=ALU.add))
                        else:
                            then(V.scalar_tensor_tensor(out=z, in0=z, scalar=w, in1=bank(7), op0=ALU.mult, op1=ALU.add))
                            if j == 1:
                                did(V.tensor_tensor(ssum[:, :], zc[:, PAD:ZW], z, ALU.add))
                            elif 1 < j < CT - 1:
                                did(V.tensor_tensor(ssum[:, :], ssum[:, :], z, ALU.add))
                            elif j == CT - 1:
                                V.tensor_tensor(ssum[:, :], ssum[:, :], z, ALU.add).then_inc(zsum_ready.h, 1)

                dve.wait_ge(col_in.h, col_in.at(layer, 1))
                gains(col[:, COL["g_mix"]:COL["g_mix"] + CT], SC_M)
                norm_half(0, SH_M, "N1")
                half_reciprocal(layer, 0, 1)
                norm_half(1, SH_M, "N1")
                z3 = zc[:, :].rearrange("p (j t) -> p j t", j=CT)
                dve.wait_ge(layer_in.h, layer_in.at(layer, 5))
                for h in range(2):
                    unit_is_done(0, 4 * h + 3)
                    for tt in range(4):
                        V.tensor_tensor(vtok[:, tt * D + h * 512:tt * D + h * 512 + 512], bank(4 * h + tt),
                                        bc[:, h * 512:h * 512 + 512], ALU.add).then_inc(dve_evac.h, 1)
                for tt in range(4):
                    for h in range(2):
                        dve.wait_ge(v_gelu.h, v_gelu.at(layer, 4 * h + tt + 1))
                        did(V.bn_stats(vbn[:, (2 * tt + h) * 6:(2 * tt + h + 1) * 6],
                                       vtok[:, tt * D + h * 512:tt * D + h * 512 + 512]))
                steps.settle()
                did(V.memset(z3[:, :, 0:PAD], 0.0))
                for tt in range(4):
                    V.bn_aggr(vmv[:, 2 * tt:2 * tt + 2], vbn[:, 12 * tt:12 * tt + 12]).then_inc(vstat_ready.h, 1)

                for p in range(8):
                    u = UNIT["A"] + 2 * p
                    dve.wait_ge(act_evac.h, act_evac.at(layer, ACT_EVAC["A"] + p + 1))
                    unit_is_done(0, u + 1)
                    V.scalar_tensor_tensor(out=z3[:, p, PAD:ZW], in0=bank((u + 1) % 4), scalar=c1(col, COL["b_in"] + BT["a"] + p),
                                           in1=tile(atmp, p % 2), op0=ALU.add, op1=ALU.mult).then_inc(dve_evac.h, 1)
                    if p == 1:
                        dve.wait_ge(std_ready.h, std_ready.at(layer, 1))
                        then(V.reciprocal(vstd[:, :], vstd[:, :]))
                    if 1 <= p <= 4:
                        for tt in (p - 1,):
                            v = vtok[:, tt * D:(tt + 1) * D]
                            then(V.tensor_scalar(v, v, c1(vmv, 2 * tt), c1(vstd, tt), ALU.subtract, ALU.mult))
                            then(V.tensor_tensor(v, v, bc[:, D:2 * D], ALU.mult))
                            V.tensor_tensor(v, v, bc[:, 2 * D:3 * D], ALU.add).then_inc(v_ready.h, 1)
                    dve.wait_ge(dve_evac.h, dve_evac.at(layer, DVE_EVAC["A"] + p + 1))
                    conv_taps(*A_TAPS[p:p + 2])

                for g in range(8):
                    dve.wait_ge(mixed_ready.h, mixed_ready.at(layer, g + 1))
                    b_s = bc[:, 3 * D + g * P:3 * D + (g + 1) * P].rearrange("p (a t) -> p a t", a=1).to_broadcast([P, 4, P])
                    V.tensor_tensor(tile(sq, g % 2).rearrange("p (n t) -> p n t", n=4),
                                    bank(4 + g % 2).rearrange("p (n t) -> p n t", n=4), b_s, ALU.add).then_inc(dve_evac.h, 1)
                    dve.wait_ge(act_evac.h, act_evac.at(layer, ACT_EVAC["U"] + g + 1))
                    dve.wait_ge(dve_evac.h, dve_evac.at(layer, DVE_EVAC["U"] + g + 1))
                    slot_is_split("U", g)
                    V.tensor_tensor(tile(dtmp, g % 2), tile(sq, g % 2), tile(atmp, g % 2), ALU.mult).then_inc(val_ready.h, 1)
                    conv_taps(U_TAPS + 5 * g, U_TAPS + 5 * (g + 1))
                    split_lo(tile(dtmp, g % 2), tile(mid_hi, OPA[0] + g), tile(mid_lo, OPA[1] + g), "U", g)

                for n in range(8):
                    u = UNIT["BRA"] + 2 * n
                    dve.wait_ge(act_evac.h, act_evac.at(layer, ACT_EVAC["BRA"] + n + 1))
                    unit_is_done(0, u + 1)
                    V.tensor_tensor(tile(merged, n), bank((u + 1) % 4), tile(atmp, n % 2), ALU.mult).then_inc(dve_evac.h, 1)
                    conv_taps(*BRA_TAPS[n:n + 2])

                then(V.memset(ptmp[:, :].rearrange("p (a t) -> p a t", a=2)[:, :, 0:WMAX - 1], 0.0))
                for k in range(8):
                    win = WINDOWS[k // 2]
                    src = ptmp[:, k % 2 * PW:(k % 2 + 1) * PW]
                    dve.wait_ge(act_evac.h, act_evac.at(layer, ACT_EVAC["P"] + k + 1))
                    have, span, b = src, 1, 0
                    while span < win:
                        span *= 2
                        lo = WMAX - 1 - (win - span)
                        nxt = wsum[:, b * PW:(b + 1) * PW]
                        then(V.tensor_tensor(nxt[:, lo:PW], have[:, lo:PW], have[:, lo - span // 2:PW - span // 2], ALU.add))
                        have, b = nxt, 1 - b
                    head = have[:, WMAX - 1:WMAX - 1 + WMAX]
                    hd = FIX["head"] + k // 2 * WMAX
                    then(V.tensor_tensor(head, head, fix[:, hd:hd + WMAX], ALU.mult))
                    slot_is_split("P", k)
                    V.scalar_tensor_tensor(out=tile(dtmp, k % 2), in0=have[:, WMAX - 1:PW], scalar=1.0 / win,
                                           in1=src[:, WMAX - 1:PW], op0=ALU.mult, op1=ALU.subtract).then_inc(val_ready.h, 1)
                    split_lo(tile(dtmp, k % 2), tile(mid_hi, OPB[0] + k), tile(mid_lo, OPB[1] + k), "P", k)

                for k in range(8):
                    unit_is_done(0, UNIT["POOL"] + k // 4)
                    if k >= 2:
                        split_lo(tile(dtmp, k % 2), tile(mid_hi, OPB[0] + k - 2), tile(mid_lo, OPB[1] + k - 2), "POOL", k - 2)
                    slot_is_split("POOL", k)
                    V.tensor_scalar(tile(dtmp, k % 2), bank(k % 7), c1(col, COL["pool_scale"] + k), None,
                                    ALU.mult).then_inc(val_ready.h, 1)
                for k in (6, 7):
                    split_lo(tile(dtmp, k % 2), tile(mid_hi, OPB[0] + k), tile(mid_lo, OPB[1] + k), "POOL", k)

                for n in range(8):
                    def branch_b():
                        u = UNIT["BRB"] + 2 * n
                        dve.wait_ge(act_evac.h, act_evac.at(layer, ACT_EVAC["BRB"] + n + 1))
                        unit_is_done(0, u + 1)
                        V.tensor_tensor(tile(atmp, n % 2), bank((u + 1) % 4), tile(atmp, n % 2), ALU.mult).then_inc(dve_evac.h, 1)
                        dve.wait_ge(dve_evac.h, dve_evac.at(layer, DVE_EVAC["BRB"] + n + 1))
                        V.tensor_tensor(tile(merged, n), tile(merged, n), tile(atmp, n % 2), ALU.add).then_inc(added.h, 1)
                        if n == 4:
                            finish(0)
                        if n < 6:
                            ada_chunk(0, n, 8)

                    if n == 6:
                        ada_chunk(0, 6, 8)
                        ada_chunk(0, 7, 8)
                        dve.wait_ge(std_ready.h, std_ready.at(layer, 2))
                        then(V.reciprocal(rstd[:, :], rstd[:, :]))
                        for k in range(CT + 2):
                            if k >= 2:
                                split_lo(tile(sq, k % 2), tile(mid_hi, OPA[0] + k - 2), tile(mid_lo, OPA[1] + k - 2), "C", k - 2)
                            if k < CT:
                                V.scalar_tensor_tensor(out=tile(dtmp, k % 2), in0=z3[:, k, PAD:ZW], scalar=c1(col, COL["conv_g"] + k),
                                                       in1=rstd[:, :], op0=ALU.mult, op1=ALU.mult).then_inc(val_ready.h, 1)
                    branch_b()
                    if n < 4:
                        conv_taps(*BRB_TAPS[n:n + 2])
                    if n == 4:
                        dve.wait_ge(stat_ready.h, stat_ready.at(layer, 1))
                        for k in range(CT + 2):
                            if k < CT:
                                V.tensor_tensor(z3[:, k, PAD:ZW], z3[:, k, PAD:ZW], bank(6), ALU.subtract).then_inc(centered.h, 1)
                            if k >= 2:
                                add_square(layer, "C", k - 2, first=k == 2)

                for n in range(8):
                    u = UNIT["BRC"] + 2 * n
                    if n % 2 == 0:
                        finish(1 + n // 2)
                    ada_chunk(0, 8 + 2 * n, 48)
                    if n % 2:
                        ada_chunk(0, 9 + 2 * n, 48)
                    dve.wait_ge(act_evac.h, act_evac.at(layer, ACT_EVAC["BRC"] + n + 1))
                    unit_is_done(0, u + 1)
                    V.tensor_tensor(tile(atmp, n % 2), bank((u + 1) % 4), tile(atmp, n % 2), ALU.mult).then_inc(dve_evac.h, 1)
                    dve.wait_ge(dve_evac.h, dve_evac.at(layer, DVE_EVAC["BRC"] + n + 1))
                    slot_is_split("BRC", n)
                    V.tensor_tensor(tile(dtmp, n % 2), tile(merged, n), tile(atmp, n % 2), ALU.add).then_inc(val_ready.h, 1)
                    split_lo(tile(dtmp, n % 2), tile(mid_hi, OPB[0] + n), tile(mid_lo, OPB[1] + n), "BRC", n)
                    if n % 2 == 0:
                        ada_chunk(0, 9 + 2 * n, 48)

                finish(5)
                for n in range(4):
                    u = UNIT["OUT"] + n
                    unit_is_done(0, u)
                    V.scalar_tensor_tensor(out=tile(x, n), in0=bank(u % 4), scalar=c1(ada, GT_M + n), in1=tile(x, n),
                                           op0=ALU.mult, op1=ALU.add).then_inc(dve_evac.h, 1)
                    if n == 3:
                        finish(6)
                    for k in ((24, 25), (26, 27), (), (28, 29))[n]:
                        ada_chunk(0, k, 48)
                    add_square(layer, "OUT", n, first=n == 0)
                for n in range(4, 8):
                    u = UNIT["OUT"] + n
                    dve.wait_ge(out_half.h, out_half.at(layer, n - 3))
                    half_update(half(bank(u % 4), 0, 0), n, 0, GT_M)
                    if n == 4:
                        gains(col[:, COL["g_ffn"]:COL["g_ffn"] + CT], SC_F)
                    add_square(layer, "OUT", n, 0)

                half_reciprocal(layer, 3, 0)

                def rest_of_x(k):
                    if k % 2:
                        n = 4 + k // 2
                        unit_is_done(0, UNIT["OUT"] + n)
                        half_update(half(bank((UNIT["OUT"] + n) % 4), 0, 1), n, 1, GT_M)
                        add_square(layer, "OUT", 4 + n, 1)

                norm_half(0, SH_F, "N2", rest_of_x)
                for k in (30, 31):
                    ada_chunk(0, k, 48)
                half_reciprocal(layer, 4, 1)
                norm_half(1, SH_F, "N2")

                def ffn_pair(i, k, m):
                    c = UNIT["FI"] + 2 * k
                    dve.wait_ge(act_evac.h, act_evac.at(layer, i * m + (ACT_EVAC["FI"] + k + 1)))
                    dve.wait_ge(unit_done.h, unit_done.at(layer, i * (2 * m) + (c + 2)))
                    dve.wait_ge(x_lo.h, x_lo.at(layer, i * m + (SPLIT["FI"] + k - 1)))
                    V.tensor_tensor(tile(dtmp, k % 2), bank((c + 1) % 4), tile(atmp, k % 2), ALU.mult).then_inc(val_ready.h, 1)
                    dve.wait_ge(x_hi.h, x_hi.at(layer, i * m + (SPLIT["FI"] + k + 1)))
                    V.tensor_tensor(mid_lo[:, ds((i * m + k) * S, S)], tile(dtmp, k % 2),
                                    mid_hi[:, ds((i * m + k) * S, S)].bitcast(f32), ALU.subtract).then_inc(x_lo.h, 1)

                with dve.Fori(0, 4) as i:
                    steps.loop, inside = i * 6, steps.n
                    n = 7
                    ada_finish(rstd[:, :], layer, i + n, i * 4 + 4 * n, layer * 48 + (i * 4 + (FIX["b_ada"] + 16 + 4 * n)))
                    for k in range(4):
                        ada_chunk(i, 32 + k, 4)
                        ffn_pair(i, k, 4)
                    assert steps.n - inside == 6
                    steps.loop, steps.n = None, inside + 4 * 6
                finish(11, settle=False)
                with dve.Fori(0, 3) as i:
                    for k in range(2):
                        ffn_pair(i, 16 + k, 2)

                steps.settle()
                for e in range(16):
                    f, n = (0, e) if e < 8 else (1, FO_B[e - 8])
                    if e == 8:
                        add_square(layer, "FO", 7, 0)
                    if e < 15:
                        dve.wait_ge(ff_bank.h, ff_bank.at(layer, e + 1))
                    else:
                        unit_is_done(0, UNITS - 1)
                    half_update(half(bank(n), 0, f), n, f, GT_F)
                    if e == 8:
                        half_reciprocal(layer, 5, 0)
                    if e % 8:
                        add_square(layer, "FO", e - 1, f, first=e % 8 == 1)
                add_square(layer, "FO", 15, 1)
                assert steps.n == DVE_STEPS, steps.n

            for f in range(2):
                if f:
                    dve.wait_ge(std_ready.h, std_ready.at(DEPTH, 0))
                    V.reciprocal(half(rstd, 0, 1), half(rstd, 0, 1)).then_inc(last_std.h, 1)
                    dve.wait_ge(last_std.h, 1)
                for k in range(CT):
                    V.scalar_tensor_tensor(out=half(x, k, f), in0=half(x, k, f), scalar=c1(fix, FIX["g_final"] + k),
                                           in1=half(rstd, 0, f), op0=ALU.mult, op1=ALU.mult).then_inc(y_ready.h, 1)

        @block.tensor
        def _(pe):
            pe.sem_inc(unit_done.h, RING)
            pe.wait_ge(fix_in.h, 16)

            def ada_sum(layer, n, acc):
                pe.wait_ge(ada_read.h, ada_read.at(layer, n)) if not (isinstance(n, int) and n == -4) else None
                pe.matmul(bank(4), ones, acc, start=True, stop=True).then_inc(ada_ready.h, 1)

            def half_sum(layer, n_sq, f, n_std=None):
                pe.wait_ge(sq_added.h, sq_added.at(layer, n_sq))
                if n_std is not None:
                    pe.wait_ge(std_ready.h, std_ready.at(layer, n_std))
                pe.matmul(half(bank(6), 0, f), mean, half(ssum, 0, f), start=True, stop=True).then_inc(stat_ready.h, 1)

            half_sum(0, 0, 0)
            half_sum(0, 0, 1, -1)
            for h in range(4):
                pe.wait_ge(pro_acc_ready.h, h + 1)
                ada_sum(0, h - 4, tile(pro_acc, h))

            with pe.Fori(0, DEPTH) as layer:
                def unit_is_split(i, c):
                    pe.wait_ge(w_lo_done.h, w_lo_done.at(layer, i * 4 + (c + 1)))

                def passes(hi, lo, whi_, wlo_, stationary):
                    for a, b in ((hi, whi_), (lo, whi_), (hi, wlo_)):
                        yield (a, b) if stationary else (b, a)

                def unit(i, c, operand, free=None, tiles=None, f=None):
                    s = c % RING
                    if free:
                        pe.wait_ge(free[0].h, free[0].at(layer, free[1]))
                    if not f:
                        unit_is_split(i, c)
                    hi, lo, th, tl = operand
                    part = tile if f is None else (lambda t, k: half(t, k, f))
                    for kt in range(8):
                        if tiles:
                            pe.wait_ge(x_lo.h, x_lo.at(layer, tiles + kt + 1))
                        w = slice(s * UC + kt * P, s * UC + (kt + 1) * P)
                        for j, (st, mv) in enumerate(passes(part(hi, th + kt), part(lo, tl + kt), whi[:, w], wlo[:, w], False)):
                            mm = pe.matmul(part(bank(s), 0), st, mv, start=(kt == 0 and j == 0), stop=(kt == 7 and j == 2))
                    if f != 0:
                        mm.then_inc(unit_done.h, 1)
                    return mm

                H = (h_hi, h_lo, 0, 0)
                opa = (mid_hi, mid_lo, *OPA)
                opb = (mid_hi, mid_lo, *OPB)

                def channel_sum(wait, n):
                    pe.wait_ge(wait.h, n)
                    pe.matmul(bank(6), mean, ssum[:, :], start=True, stop=True).then_inc(stat_ready.h, 1)

                def v_unit(h, q, tts, ready=None):
                    for j in range(2):
                        kt = 2 * q + j
                        if ready is not None:
                            pe.wait_ge(x_lo.h, x_lo.at(layer, SPLIT["N1"] + ready + kt + 1))
                        w = slice(q * UC + j * 512, q * UC + (j + 1) * 512)
                        for tt in tts:
                            t = slice(kt * S + tt * P, kt * S + (tt + 1) * P)
                            for m, (st, mv) in enumerate(passes(h_hi[:, t], h_lo[:, t], whi[:, w], wlo[:, w], True)):
                                mm = pe.matmul(bank(4 * h + tt), st, mv, start=(kt == 0 and m == 0), stop=(kt == 7 and m == 2))
                    return mm

                for q in range(4):
                    unit_is_split(0, q)
                    v_unit(0, q, (0, 1), 0)
                for q in range(4):
                    v_unit(0, q, (2, 3), CT).then_inc(unit_done.h, 1)
                for q in range(4):
                    unit_is_split(0, 4 + q)
                    v_unit(1, q, range(4)).then_inc(unit_done.h, 1)

                for c in range(4):
                    unit(0, UNIT["A"] + c, H, free=(dve_evac, DVE_EVAC["V"] + c + 1))
                with pe.Fori(0, 3) as i:
                    for c in range(4):
                        f = (act_evac, i * 2 + (ACT_EVAC["A"] + c // 2 + 1)) if c % 2 == 0 else (dve_evac, i * 2 + (DVE_EVAC["A"] + c // 2 + 1))
                        unit(i, UNIT["A"] + 4 + c, H, free=f)

                pe.wait_ge(ws_masked.h, ws_masked.at(layer, 1))
                for g in range(8):
                    if g == 0:
                        pe.wait_ge(v_ready.h, v_ready.at(layer, 4))
                    pe.wait_ge(dve_evac.h, dve_evac.at(layer, DVE_EVAC["V"] + 5 + g if g < 2 else DVE_EVAC["U"] + g - 1))
                    for tt in range(4):
                        mm = pe.matmul(psum[:, (4 + g % 2) * 512 + tt * P:(4 + g % 2) * 512 + (tt + 1) * P],
                                       vtok[:, tt * D + g * P:tt * D + (g + 1) * P], wsT[:, g * P:(g + 1) * P], start=True, stop=True)
                    mm.then_inc(mixed_ready.h, 1)
                    if g < 4:
                        f = (act_evac, ACT_EVAC["A"] + 7 + g // 2) if g % 2 == 0 else (dve_evac, DVE_EVAC["A"] + 7 + g // 2)
                    else:
                        f = (act_evac, ACT_EVAC["U"] + g - 3)
                    unit(0, UNIT["U"] + g, H, free=f)

                def branch(stage, body, operand, ready, prev=None, behind={}):
                    i, k = body
                    for c in range(4):
                        if prev:
                            f = prev[c]
                        elif c % 2 == 0:
                            f = (act_evac, i * 2 + (ACT_EVAC[stage] + 2 * (k - 1) + c // 2 + 1))
                        else:
                            f = (dve_evac, i * 2 + (DVE_EVAC[stage] + 2 * (k - 1) + c // 2 + 1))
                        first = k == 0 and c == 1
                        unit(i, UNIT[stage] + 4 * k + c, H if c % 2 == 0 else operand, free=f, tiles=ready if first else None)
                        if c in behind:
                            behind[c]()

                branch("BRA", (0, 0), opa, SPLIT["U"], [(act_evac, ACT_EVAC["U"] + 5 + c) for c in range(4)])
                with pe.Fori(0, 3) as i:
                    branch("BRA", (i, 1), opa, SPLIT["U"])

                for c in range(4):
                    f = (act_evac, ACT_EVAC["BRA"] + 7 + c // 2) if c % 2 == 0 else (dve_evac, DVE_EVAC["BRA"] + 7 + c // 2)
                    unit(0, UNIT["P"] + c, H, free=f)
                for c in range(4):
                    unit(0, UNIT["P"] + 4 + c, H, free=(act_evac, ACT_EVAC["P"] + c + 1))

                for q in range(2):
                    c = UNIT["POOL"] + q
                    unit_is_split(0, c)
                    for g in (2 * q, 2 * q + 1):
                        pe.wait_ge(x_lo.h, x_lo.at(layer, SPLIT["P"] + 2 * g + 2))
                        for nt in range(2):
                            k = 2 * g + nt
                            if k < 4:
                                pe.wait_ge(act_evac.h, act_evac.at(layer, ACT_EVAC["P"] + 5 + k))
                            elif k < 6:
                                pe.wait_ge(dve_evac.h, dve_evac.at(layer, DVE_EVAC["U"] + 3 + k))
                            elif k == 7:
                                pe.wait_ge(val_ready.h, val_ready.at(layer, SPLIT["POOL"] + 1))
                            for kt in range(2):
                                o = (c % RING) * UC + (g % 2) * 512 + kt * 256 + nt * P
                                hi, lo = tile(mid_hi, OPB[0] + 2 * g + kt), tile(mid_lo, OPB[1] + 2 * g + kt)
                                for m, (st, mv) in enumerate(passes(hi, lo, whi[:, o:o + P], wlo[:, o:o + P], False)):
                                    mm = pe.matmul(bank(k % 7), st, mv, start=(kt == 0 and m == 0), stop=(kt == 1 and m == 2))
                    mm.then_inc(unit_done.h, 1)

                branch("BRB", (0, 0), opb, SPLIT["POOL"], [(val_ready, SPLIT["POOL"] + n) for n in (3, 4, 8, 2)])
                branch("BRB", (0, 1), opb, SPLIT["POOL"])

                def mean_sum():
                    channel_sum(zsum_ready, zsum_ready.at(layer, 1))

                def variance_sum():
                    channel_sum(sq_added, sq_added.at(layer, SQ["C"] + 8))

                def half_vector(n):
                    def f():
                        pe.wait_ge(ada_used.h, ada_used.at(layer, 4 * n + 4))
                        ada_sum(layer, n, ada_acc[:, :])
                    return f

                branch("BRB", (0, 2), opb, SPLIT["POOL"], behind={0: half_vector(0), 1: mean_sum, 3: variance_sum})
                branch("BRB", (0, 3), opb, SPLIT["POOL"])

                for k in range(4):
                    prev = None if k else [(act_evac, ACT_EVAC["BRB"] + 7), (dve_evac, DVE_EVAC["BRB"] + 7),
                                           (act_evac, ACT_EVAC["BRB"] + 8), (dve_evac, DVE_EVAC["BRB"] + 8)]
                    branch("BRC", (0, k), opa, SPLIT["C"], prev, behind={0: half_vector(1 + k)})

                half_vector(5)()
                for c in range(4):
                    f = (act_evac, ACT_EVAC["BRC"] + 7 + c // 2) if c % 2 == 0 else (dve_evac, DVE_EVAC["BRC"] + 7 + c // 2)
                    unit(0, UNIT["OUT"] + c, opb, free=f, tiles=SPLIT["BRC"] if c == 0 else None)
                    if c == 2:
                        half_vector(6)()
                for c in range(4, 8):
                    unit(0, UNIT["OUT"] + c, opb, free=(dve_evac, DVE_EVAC["OUT"] + c - 3), f=0).then_inc(out_half.h, 1)
                for c in range(4, 8):
                    unit(0, UNIT["OUT"] + c, opb, free=(dve_evac, DVE_EVAC["OUT"] + c + 1), f=1)
                    if c == 4:
                        half_sum(layer, SQ["OUT"] + 8, 0)

                def ffn_units(i, m, k):
                    for c in range(4):
                        if c % 2 == 0:
                            f = (act_evac, i * (2 * m) + (ACT_EVAC["FI"] + 2 * k - 1 + c // 2))
                        else:
                            f = (val_ready, i * (2 * m) + (SPLIT["FI"] + 2 * k - 1 + c // 2))
                        unit(i * m if m > 1 else i, UNIT["FI"] + 4 * k + c, H, free=f)

                for c in range(4):
                    unit(0, UNIT["FI"] + c, H, free=(dve_evac, DVE_EVAC["OUT"] + 9 + c), tiles=SPLIT["N2"] if c == 0 else None, f=0)
                    if c == 1:
                        half_sum(layer, SQ["OUT"] + 12, 1, 3)
                for c in range(4):
                    unit(0, UNIT["FI"] + c, H, tiles=SPLIT["N2"] + CT if c == 0 else None, f=1)
                    if c == 2:
                        half_vector(7)()
                ffn_units(0, 1, 1)
                with pe.Fori(0, 3) as i:
                    pe.wait_ge(ada_used.h, ada_used.at(layer, i * 4 + 36))
                    ada_sum(layer, i + 8, ada_acc[:, :])
                    ffn_units(i, 2, 2)
                    ffn_units(i, 2, 3)
                pe.wait_ge(ada_used.h, ada_used.at(layer, 48))
                ada_sum(layer, 11, ada_acc[:, :])
                with pe.Fori(0, 3) as i:
                    ffn_units(i, 1, 8)

                def ff_matmuls(kt, s, n, first, last, f=None):
                    w = slice(s * UC + n * P, s * UC + (n + 1) * P)
                    t = ds(kt * S, S) if f is None else slice(kt * S + f * HS, kt * S + (f + 1) * HS)
                    for m, (st, mv) in enumerate(passes(mid_hi[:, t], mid_lo[:, t], whi[:, w], wlo[:, w], False)):
                        mm = pe.matmul(bank(n) if f is None else half(bank(n), 0, f), st, mv, start=(first and m == 0), stop=(last and m == 2), skip_group_check=(f == 1))
                    return mm

                def ff_unit(i, k, first=False):
                    c = UNIT["FO"] + k
                    unit_is_split(i, c)
                    pe.wait_ge(x_lo.h, x_lo.at(layer, i * 4 + (SPLIT["FI"] + k + 1)))
                    for n in range(8):
                        if first and n < 4:
                            order = (n - UNIT["FO"]) % 4
                            e = (act_evac, ACT_EVAC["FI"] + FT - 1 + order // 2) if order % 2 == 0 else (val_ready, SPLIT["FI"] + FT - 1 + order // 2)
                            pe.wait_ge(e[0].h, e[0].at(layer, e[1]))
                        if first and n == 4:
                            pe.wait_ge(ada_read.h, ada_read.at(layer, 12))
                        mm = ff_matmuls(i * 4 + k, c % RING, n, first, False)
                    mm.then_inc(unit_done.h, 1)

                ff_unit(0, 0, first=True)
                ff_unit(0, 1)
                with pe.Fori(0, 4) as i:
                    for k in range(4):
                        ff_unit(i, 2 + k)
                for k in range(4):
                    unit_is_split(0, UNITS - 4 + k)
                pe.wait_ge(x_lo.h, x_lo.at(layer, SPLIT["FI"] + FT))
                def ff_half(n, ks, f):
                    for k in ks:
                        mm = ff_matmuls(FT - 4 + k, k, n, False, k == 3, f)
                    return mm

                for n in range(8):
                    ff_half(n, range(4), 0).then_inc(ff_bank.h, 1)
                pe.wait_ge(dve_evac.h, dve_evac.at(layer, DVE_EVAC["FO"] + 7))
                ff_half(FO_B[0], range(4), 1).then_inc(ff_bank.h, 1)
                for k in range(2):
                    for n in FO_B[1:]:
                        if k == 0 and n == 7:
                            pe.wait_ge(dve_evac.h, dve_evac.at(layer, DVE_EVAC["FO"] + 8))
                        mm = ff_half(n, (k,), 1)
                    mm.then_inc(unit_done.h, 1)
                    if k == 0:
                        pe.wait_ge(dve_evac.h, dve_evac.at(layer, DVE_EVAC["FO"] + 9))
                        half_sum(layer, SQ["FO"] + 8, 0)
                for n in FO_B[1:]:
                    mm = ff_half(n, (2,), 1)
                    if n == FO_B[-1]:
                        mm.then_inc(unit_done.h, 1)
                    mm = ff_half(n, (3,), 1)
                    mm.then_inc(unit_done.h if n == FO_B[-1] else ff_bank.h, 1)
                half_sum(layer, SQ["FO"] + 16, 1, 5)


def _tiles(w, n0, n):
    k = w.shape[0] // P
    return w[:, n0:n0 + n * P].reshape(k, P, n, P).transpose(2, 1, 0, 3).reshape(n, P, k * P)


def _pairs(a, b):
    return np.stack([a, b], axis=1).reshape(-1, P, UC)


def _columns(v):
    return v.reshape(-1, P).T


def kernel(x, c, w_ada, b_ada, g_mix, w_in, b_in, sgu_ln_g, sgu_ln_b, sgu_w_s, sgu_b_s, w_pa, pool_w, pool_scale,
           w_pb, conv_w, conv_b, conv_ln_g, conv_ln_b, w_pc, w_out, g_ffn, w_ffn_in, w_ffn_out, g_final):
    import concourse.bacc as bacc
    from concourse import mybir as _mybir
    from concourse.bass_utils import run_bass_kernel_spmd as run

    (x, c, w_ada, b_ada, g_mix, w_in, b_in, sgu_ln_g, sgu_ln_b, sgu_w_s, sgu_b_s, w_pa, pool_w, pool_scale,
     w_pb, conv_w, conv_b, conv_ln_g, conv_ln_b, w_pc, w_out, g_ffn, w_ffn_in, w_ffn_out, g_final) = (
        np.asarray(a) for a in (x, c, w_ada, b_ada, g_mix, w_in, b_in, sgu_ln_g, sgu_ln_b, sgu_w_s, sgu_b_s, w_pa,
                                pool_w, pool_scale, w_pb, conv_w, conv_b, conv_ln_g, conv_ln_b, w_pc, w_out, g_ffn,
                                w_ffn_in, w_ffn_out, g_final))

    stream = []
    for l in range(DEPTH):
        wi = w_in[l]
        for half in range(2):
            v = wi[:, BT["v"] * P + half * 512:BT["v"] * P + half * 512 + 512]
            stream.append(v.reshape(4, 2, P, 512).transpose(0, 2, 1, 3).reshape(4, P, UC))
        stream.append(_pairs(_tiles(wi, BT["ag"] * P, 8), _tiles(wi, BT["a"] * P, 8)))
        stream.append(_tiles(wi, BT["u"] * P, 8))
        stream.append(_pairs(_tiles(wi, BT["gate"] * P, 8), _tiles(w_pa[l], 0, 8)))
        stream.append(_tiles(wi, BT["p"] * P, 8))
        stream.append(pool_w[l].reshape(2, 2, 2, P, 256).transpose(0, 3, 1, 2, 4).reshape(2, P, UC))
        stream.append(_pairs(_tiles(wi, (BT["gate"] + 8) * P, 8), _tiles(w_pb[l], 0, 8)))
        stream.append(_pairs(_tiles(wi, (BT["gate"] + 16) * P, 8), _tiles(w_pc[l], 0, 8)))
        stream.append(_tiles(w_out[l], 0, 8))
        stream.append(_pairs(_tiles(w_ffn_in[l], 0, FT), _tiles(w_ffn_in[l], D_FF, FT)))
        stream.append(w_ffn_out[l].reshape(FT, P, D))
    stream.append(stream[0][:RAW])
    weights = np.concatenate(stream)

    a = w_ada.reshape(DEPTH, 4, 2, P, 6, 2, 512).transpose(0, 4, 5, 1, 3, 2, 6).reshape(DEPTH, 6, 8, P, UC)
    b = b_ada.reshape(DEPTH, 6, D)
    order = [(0, 0), (0, 1)]
    for l in range(DEPTH):
        order += [(l, j) for j in range(2, 6)] + [((l + 1) % DEPTH, j) for j in (0, 1)]
    ada_stream = np.concatenate([a[l, j] for l, j in order])
    b_cols = np.concatenate([_columns(b[l, j]) for l, j in order], axis=1)

    cols = np.stack([np.concatenate([
        _columns(g_mix[l]), _columns(b_in[l]), _columns(g_ffn[l]), _columns(conv_b[l]), _columns(conv_ln_g[l]),
        _columns(conv_ln_b[l]), _columns(pool_scale[l]),
        conv_w[l].reshape(TAPS, CT, P).transpose(2, 1, 0).reshape(P, CT * TAPS)], axis=1) for l in range(DEPTH)])
    rows = np.concatenate([np.stack([b_in[l][BT["v"] * P:BT["v"] * P + D], sgu_ln_g[l], sgu_ln_b[l],
                                     sgu_b_s[l].reshape(-1)]) for l in range(DEPTH)])
    ws = sgu_w_s.transpose(0, 3, 1, 2).reshape(DEPTH, P, 8 * P)
    head = np.array([[win / min(t + 1, win) for t in range(WMAX)] for win in WINDOWS], np.float32).reshape(1, -1)
    f = np.float32
    fixed = np.concatenate([b_cols, _columns(g_final), _columns(c), np.full((P, 1), EPS, f), np.repeat(head, P, 0),
                            np.eye(P, dtype=f), np.ones((P, P), f), np.full((P, P), 1.0 / D, f)], axis=1)
    xT = x[0].reshape(S, CT, P).transpose(2, 1, 0).reshape(P, CT * S)

    nc = bacc.Bacc("TRN2", target_bir_lowering=False, num_devices=1, dynamic_dma_scratch_size=1024)
    arrays, args = {}, []
    for name, arr in (("xT", xT), ("fixed", fixed), ("cols", cols), ("rows", rows), ("ws", ws), ("w_ada", ada_stream),
                      ("weights", weights)):
        arrays[name + "_in"] = np.ascontiguousarray(arr)
        args.append(nc.dram_tensor(name + "_in", arr.shape, _mybir.dt.float32, kind="ExternalInput").ap())
    args.append(nc.dram_tensor("y_out", (P, CT * S), _mybir.dt.float32, kind="ExternalOutput").ap())
    trunk(nc, *args)
    r = run(nc, [arrays], core_ids=[0])
    y = r.results[0]["y_out"]
    return np.ascontiguousarray(y.reshape(P, CT, S).transpose(2, 1, 0).reshape(1, S, D))
```

```python
import concourse.bass as bass
from concourse import mybir
import numpy as np
from contextlib import ExitStack

P = 128
D = 1024
S = 512
HS = S // 2
DEPTH = 2
CT = D // P
D_FF = 2816
FT = D_FF // P
TAPS = 31
PAD = TAPS - 1
WINDOWS = (2, 4, 8, 16)
WMAX = max(WINDOWS)
BRC_BANK = 5
EPS = 1e-6

UC = 1024
UNIT, at = {}, 0
for stage, n in (("V", 8), ("A", 16), ("U", 8), ("BRA", 16), ("P", 8), ("POOL", 2), ("BRB", 16),
                 ("BRC", 16), ("OUT", 8), ("FI", 2 * FT), ("FO", FT)):
    UNIT[stage] = at
    at += n
UNITS = at
RING = 4
RAW = 2

def bases(*counts):
    out, n = {}, 0
    for name, k in counts:
        out[name] = n
        n += k
    return out, n


ACT_EVAC, N_ACT_EVAC = bases(("A", 8), ("U", 8), ("BRA", 8), ("P", 8), ("BRB", 8), ("BRC", 8), ("FI", FT))
DVE_EVAC, N_DVE_EVAC = bases(("V", 8), ("A", 8), ("U", 8), ("BRA", 8), ("BRB", 8), ("BRC", 8), ("OUT", 12), ("FO", 16))
SPLIT, N_SPLIT = bases(("N1", 16), ("U", 8), ("P", 8), ("POOL", 8), ("C", 8), ("BRC", 8), ("N2", 16), ("FI", FT))
SQ, N_SQ = bases(("C", 8), ("OUT", 12), ("FO", 16))
FO_B = (6, 0, 1, 2, 3, 4, 5, 7)
ADA_HALVES = 12
PRO_DVE = 5
ADA_CHUNKS = 4 * ADA_HALVES

A_TAPS = (0, 12, 20, 28, 36, 44, 57, 70, 74)
U_TAPS = A_TAPS[-1]
BRA_TAPS = (114, 127, 140, 153, 166, 179, 192, 205, 210)
P_TAPS = (210, 212, 214, 216, 218, 219, 220, 221, 222)
BRB_TAPS = (222, 229, 236, 242, 8 * TAPS)
DVE_STEPS = 382

COL, N_COL = bases(("g_mix", 8), ("b_in", 64), ("g_ffn", 8), ("conv_b", 8), ("conv_g", 8), ("conv_lb", 8),
                   ("pool_scale", 8), ("conv_w", 8 * TAPS))
FIX, N_FIX = bases(("b_ada", 48 * DEPTH + 16), ("g_final", 8), ("c", 8), ("eps", 1), ("head", 4 * WMAX),
                   ("ident", P), ("ones", P), ("mean", P))
BT = {"u": 0, "v": 8, "p": 16, "a": 24, "ag": 32, "gate": 40}
GT_M, SH_F, SC_F, GT_F, SH_M, SC_M = (8 * j for j in range(6))


class Sem:

    def __init__(self, handle, per_layer=0, start=0, unit=1):
        self.h, self.per, self.start, self.unit = handle, per_layer, start, unit

    def at(self, layer, n):
        assert not isinstance(n, int) or n + self.start > 0
        return (layer * self.per + (n + self.start)) * self.unit


class Steps:

    def __init__(self, eng, sem):
        self.eng, self.sem, self.layer, self.n, self.loop = eng, sem, 0, 0, None

    def did(self, ins):
        ins.then_inc(self.sem.h, 1)
        self.n += 1

    def settle(self):
        n = self.n if self.loop is None else self.loop + self.n
        self.eng.wait_ge(self.sem.h, self.sem.at(self.layer, n))


def trunk(nc, xT, fixed, cols, rows, ws, w_ada, weights, out):
    f32, f32r = mybir.dt.float32, mybir.dt.float32r
    ALU, ACT = mybir.AluOpType, mybir.ActivationFunctionType
    AX = mybir.AxisListType
    ds = bass.ds

    top = [1152]

    def aligned(n):
        return -(-n // 32) * 32

    def place(name, width, dt=f32, offset=None):
        if offset is None:
            offset = top[0]
            top[0] += aligned(4 * width)
        return nc.alloc_sbuf_tensor_at(name, [P, width], dt, offset=offset), offset

    x, _ = place("x", CT * S)
    raw, _ = place("raw", RAW * UC)
    whi, _ = place("whi", RING * UC, f32r)
    wlo, _ = place("wlo", RING * UC, f32r)
    h_hi, h_at = place("h_hi", CT * S, f32r)
    h_lo, _ = place("h_lo", CT * S, f32r)
    mid_lo, lo_at = place("mid_lo", FT * S, f32r)
    mid_hi, hi_at = place("mid_hi", FT * S, f32r)
    merged, merged_at = place("merged", CT * S)
    ada_raw, _ = place("ada_raw", 2 * UC)
    ada_acc, _ = place("ada_acc", 512)
    atmp, _ = place("atmp", 2 * S)
    dtmp, _ = place("dtmp", 2 * S)
    sq, _ = place("sq", 2 * S)
    ssum, _ = place("ssum", S)
    rstd, _ = place("rstd", S)
    col, _ = place("col", N_COL)
    fix, _ = place("fix", N_FIX)
    ada, _ = place("ada", 48)
    gain, _ = place("gain", CT)
    cact, _ = place("cact", CT)
    vbn, _ = place("vbn", 4 * 2 * 6)
    vmv, _ = place("vmv", 4 * 2)
    vstd, _ = place("vstd", 4)
    FREE = FT - 2 * CT
    OPA, OPB = (FREE, 0), (FREE + CT, CT)
    gap = lo_at + 4 * 2 * CT * S
    assert gap + 4 * 2 * FREE * S == hi_at + 4 * FREE * S
    ZW = PAD + S
    ws_at = gap + aligned(4 * CT * ZW)
    pro_at = ws_at + 4 * 8 * P
    assert pro_at <= gap + 4 * 2 * FREE * S
    zc, _ = place("zc", CT * ZW, offset=gap)
    wsT, _ = place("wsT", 8 * P, offset=ws_at)
    vtok, _ = place("vtok", 4 * D, offset=lo_at + 4 * CT * S)
    PW = WMAX - 1 + S
    ptmp, _ = place("ptmp", 2 * PW, offset=lo_at)
    wsum, _ = place("wsum", 2 * PW, offset=lo_at + aligned(4 * 2 * PW))
    bc, _ = place("bc", 4 * D, offset=merged_at)
    pro_raw = [place(f"pro_raw{h}", 4 * UC, offset=lo_at + 4 * 4 * UC * h if h < 3 else pro_at)[0]
               for h in range(4)]
    pro_acc, _ = place("pro_acc", 4 * 512, offset=h_at)
    psum = nc.alloc_psum_tensor("psum", [P, 8 * 512], f32)

    def bank(b):
        return psum[:, 512 * b:512 * b + 512]

    def tile(t, k, w=S):
        return t[:, k * w:(k + 1) * w]

    def half(t, k, f, w=S):
        return t[:, k * w + f * HS:k * w + (f + 1) * HS]

    def half3(t, k0, k1, f):
        return t[:, :].rearrange("p (k t) -> p k t", k=CT)[:, k0:k1, f * HS:(f + 1) * HS]

    def c1(t, k):
        return t[:, k:k + 1]

    ident = fix[:, FIX["ident"]:FIX["ident"] + P]
    ones = fix[:, FIX["ones"]:FIX["ones"] + P]
    mean = fix[:, FIX["mean"]:FIX["mean"] + P]
    eps = c1(fix, FIX["eps"])

    ctx = ExitStack()
    with ctx:
        def sem(name, per_layer=0, start=0, unit=1):
            return Sem(ctx.enter_context(nc.semaphore(name)), per_layer, start, unit)

        fix_in, x_in = sem("fix_in"), sem("x_in")
        pro_in = [sem(f"pro_in{h}") for h in range(7)]
        raw_in = [sem(f"raw_in{s}", UNITS // RAW, unit=16) for s in range(RAW)]
        ada_in = [sem(f"ada_in{s}", ADA_CHUNKS // 2, unit=16) for s in range(2)]
        col_in = sem("col_in", 1, unit=16)
        layer_in = sem("layer_in", 5, unit=16)
        out_done = sem("out_done")
        w_hi_done = sem("w_hi_done", UNITS)
        act_evac = sem("act_evac", N_ACT_EVAC)
        x_hi = sem("x_hi", N_SPLIT)
        sq_ready = sem("sq_ready", N_SQ, 8)
        std_ready = sem("std_ready", 6, 1)
        v_gelu = sem("v_gelu", 8)
        silu_ready = sem("silu_ready", 8)
        c_ready = sem("c_ready")
        w_lo_done = sem("w_lo_done", UNITS, RAW)
        ws_masked = sem("ws_masked", 1)
        unit_done = sem("unit_done", UNITS, RING)
        mixed_ready = sem("mixed_ready", 8)
        stat_ready = sem("stat_ready", 6, 1)
        ada_ready = sem("ada_ready", ADA_HALVES, 4)
        ff_bank = sem("ff_bank", 15)
        out_half = sem("out_half", 4)
        dve_evac = sem("dve_evac", N_DVE_EVAC)
        val_ready = sem("val_ready", N_SPLIT)
        x_lo = sem("x_lo", N_SPLIT)
        sq_added = sem("sq_added", N_SQ, 8 + 2)
        zsum_ready = sem("zsum_ready", 1)
        centered = sem("centered", 8)
        vstat_ready = sem("vstat_ready", 4)
        v_ready = sem("v_ready", 4)
        added = sem("added", 8)
        ada_used = sem("ada_used", ADA_CHUNKS, 2)
        ada_read = sem("ada_read", ADA_HALVES, 4)
        pro_acc_ready = sem("pro_acc_ready")
        dve_step = sem("dve_step", DVE_STEPS)
        last_std = sem("last_std")
        y_ready = sem("y_ready")

        block = ctx.enter_context(nc.Block())

        @block.sync
        def _(sp):
            sp.dma_start(fix[:, :], fixed[:, :]).then_inc(fix_in.h, 16)
            for h in range(3):
                if h == 2:
                    sp.dma_start(x[:, :], xT[:, :]).then_inc(x_in.h, 16)
                sp.dma_start(pro_raw[h][:, :].rearrange("p (c n) -> p c n", c=4),
                             w_ada[4 * h:4 * h + 4, :, :].rearrange("c p n -> p c n")).then_inc(pro_in[h].h, 16)
            for c in range(4):
                if c == 2:
                    for u in range(RAW):
                        sp.dma_start(tile(raw, u, UC), weights[u, :, :]).then_inc(raw_in[u].h, 16)
                sp.dma_start(tile(pro_raw[3], c, UC), w_ada[12 + c, :, :]).then_inc(pro_in[3 + c].h, 16)

            with sp.Fori(0, DEPTH) as layer:
                sp.dma_start(col[:, :], cols[ds(layer, 1), :, :].rearrange("a p n -> p (a n)")).then_inc(col_in.h, 16)

                def load_unit(i, c):
                    sp.wait_ge(w_lo_done.h, w_lo_done.at(layer, i * 4 + (c - RAW + 1)))
                    sp.dma_start(tile(raw, c % RAW, UC), weights[ds(layer * UNITS + (i * 4 + c), 1), :, :]
                                 .rearrange("a p n -> p (a n)")).then_inc(raw_in[c % RAW].h, 16)

                def load_ada(c):
                    i, k, m = c
                    sp.wait_ge(ada_used.h, ada_used.at(layer, i * m + (k - 1)))
                    sp.dma_start(tile(ada_raw, k % 2, UC), w_ada[ds(layer * ADA_CHUNKS + (i * m + (k + 16)), 1), :, :]
                                 .rearrange("a p n -> p (a n)")).then_inc(ada_in[k % 2].h, 16)

                for c in (2, 3):
                    load_unit(0, c)
                for r in range(4):
                    sp.dma_start(tile(bc, r, D), rows[ds(layer * 4 + r, 1), :].to_broadcast([P, D])).then_inc(layer_in.h, 16)
                sp.dma_start(wsT[:, :], ws[ds(layer, 1), :, :].rearrange("a p n -> p (a n)")).then_inc(layer_in.h, 16)
                with sp.Fori(0, 14) as i:
                    for c in range(4):
                        load_unit(i, 4 + c)
                with sp.Fori(0, 3) as i:
                    for c in range(4):
                        if c % 2 == 0:
                            load_ada((i, c // 2, 2))
                        load_unit(i, 60 + c)
                for c in range(72, 78):
                    if c in (74, 76):
                        load_ada((0, 6 + (c - 74) // 2, 4))
                    load_unit(0, c)
                with sp.Fori(0, 4) as i:
                    for c in range(4):
                        load_ada((i, 8 + c, 4))
                        load_unit(i, 78 + c)
                for c, chunks in ((94, (24,)), (95, (25, 26)), (96, (27,)), (97, (28, 29)), (98, (30, 31)), (99, ()),
                                  (100, ()), (101, ())):
                    for k in chunks:
                        load_ada((0, k, 4))
                    load_unit(0, c)
                with sp.Fori(0, 8) as i:
                    for c in range(4):
                        if c % 2 == 0:
                            load_ada((i, 32 + c // 2, 2))
                        load_unit(i, 102 + c)
                with sp.Fori(0, 8) as i:
                    for c in range(4):
                        load_unit(i, 134 + c)

            pieces = ((0, 0, 4), (0, 4, 8), (1, 0, 4), (1, 4, 6), (1, 6, 8))
            for f, k0, k1 in pieces:
                sp.wait_ge(y_ready.h, f * CT + k1)
                sp.dma_start(half3(out, k0, k1, f), half3(x, k0, k1, f)).then_inc(out_done.h, 16)
            sp.wait_ge(out_done.h, 16 * len(pieces))

        @block.gpsimd
        def _(pool):
            pool.sem_inc(w_lo_done.h, RAW)
            pool.sem_inc(sq_added.h, 2)

            def low_part(i, c, layer):
                s = c % RING
                pool.wait_ge(w_hi_done.h, w_hi_done.at(layer, i * 4 + (c + 1)))
                pool.tensor_tensor(tile(wlo, s, UC), tile(raw, c % RAW, UC), tile(whi, s, UC).bitcast(f32),
                                   ALU.subtract).then_inc(w_lo_done.h, 1)

            for k in range(CT):
                pool.wait_ge(sq_ready.h, k + 1)
                if k == 0:
                    pool.tensor_copy(ssum[:, :], tile(sq, 0)).then_inc(sq_added.h, 1)
                else:
                    pool.wait_ge(sq_added.h, k + 2)
                    pool.tensor_tensor(ssum[:, :], ssum[:, :], tile(sq, k % 2), ALU.add).then_inc(sq_added.h, 1)
            for c in range(2):
                low_part(0, c, 0)
            with pool.Fori(0, DEPTH) as layer:
                for c in range(2, 9):
                    low_part(0, c, layer)
                pool.wait_ge(layer_in.h, layer_in.at(layer, 5))
                low_part(0, 9, layer)
                w3 = wsT[:, :].rearrange("p (g t) -> p g t", g=8)
                pool.affine_select(out=w3, in_=w3, compare_op=ALU.is_ge, fill=0.0, base=0,
                                   pattern=[[0, 8], [1, P]], channel_multiplier=-1).then_inc(ws_masked.h, 1)
                with pool.Fori(0, (UNITS - 12) // 4) as i:
                    for c in range(4):
                        low_part(i, 10 + c, layer)
                low_part(0, UNITS - 2, layer)
                low_part(0, UNITS - 1, layer)

                def add_squares(f, es):
                    total = half(ssum, 0, f)
                    for e in es:
                        n = SQ["FO"] + e
                        pool.wait_ge(sq_ready.h, sq_ready.at(layer, n + 1))
                        if e % 8 == 1:
                            pool.tensor_tensor(total, half(sq, 0, f), half(sq, 1, f), ALU.add).then_inc(sq_added.h, 2)
                        else:
                            pool.wait_ge(sq_added.h, sq_added.at(layer, n))
                            pool.tensor_tensor(total, total, half(sq, e % 2, f), ALU.add).then_inc(sq_added.h, 1)

                add_squares(0, range(1, 8))
                low_part(0, UNITS, layer)
                add_squares(1, range(9, 16))
                low_part(0, UNITS + 1, layer)

        @block.scalar
        def _(act):
            A = nc.scalar.activation

            act.wait_ge(fix_in.h, 16)
            A(cact[:, :], fix[:, FIX["c"]:FIX["c"] + CT], ACT.Silu).then_inc(c_ready.h, 1)
            act.wait_ge(x_in.h, 16)
            for k in range(CT):
                if k >= 2:
                    act.wait_ge(sq_added.h, k + 1)
                A(tile(sq, k % 2), tile(x, k), ACT.Square).then_inc(sq_ready.h, 1)

            def std(layer, n_stat, f):
                act.wait_ge(stat_ready.h, stat_ready.at(layer, n_stat))
                A(half(rstd, 0, f), half(bank(6), 0, f), ACT.Sqrt, bias=eps).then_inc(std_ready.h, 1)

            def weight_hi(i, c, layer):
                act.wait_ge(raw_in[c % RAW].h, raw_in[c % RAW].at(layer, i * 2 + (c // 2 + 1)))
                act.wait_ge(unit_done.h, unit_done.at(layer, i * 4 + (c - RING + 1)))
                nc.scalar.copy(tile(whi, c % RING, UC), tile(raw, c % RAW, UC)).then_inc(w_hi_done.h, 1)

            std(0, 0, 0)
            weight_hi(0, 0, 0)
            weight_hi(0, 1, 0)

            with act.Fori(0, DEPTH) as layer:

                def unit_is_done(i, c):
                    act.wait_ge(unit_done.h, unit_done.at(layer, i * 4 + (c + 1)))

                def split_hi(hi, t, stage, k):
                    act.wait_ge(val_ready.h, val_ready.at(layer, SPLIT[stage] + k + 1))
                    nc.scalar.copy(tile(hi, t), tile(dtmp, k % 2)).then_inc(x_hi.h, 1)

                def norm_half(f, shift, stage, unit=None):
                    for k in range(CT):
                        e = f * CT + k
                        if k == 5 and unit is not None:
                            weight_hi(0, unit, layer)
                        act.wait_ge(val_ready.h, val_ready.at(layer, SPLIT[stage] + e + 1))
                        A(half(h_hi, k, f), tile(dtmp, e % 4, HS), ACT.Identity, bias=c1(ada, shift + k)).then_inc(x_hi.h, 1)

                def square(src, stage, e, f=None):
                    act.wait_ge(sq_added.h, sq_added.at(layer, SQ[stage] + e - 1))
                    A(tile(sq, e % 2) if f is None else half(sq, e % 2, f), src, ACT.Square).then_inc(sq_ready.h, 1)

                act.wait_ge(col_in.h, col_in.at(layer, 1))
                norm_half(0, SH_M, "N1", 2)
                std(layer, 1, 1)
                weight_hi(0, 3, layer)
                norm_half(1, SH_M, "N1")

                act.wait_ge(layer_in.h, layer_in.at(layer, 5))
                for u in range(8):
                    weight_hi(0, u + 4, layer)
                    if u % 4 == 3:
                        for tt in range(4):
                            n = u // 4 * 4 + tt
                            v = vtok[:, tt * D + u // 4 * 512:tt * D + u // 4 * 512 + 512]
                            act.wait_ge(dve_evac.h, dve_evac.at(layer, DVE_EVAC["V"] + n + 1))
                            A(v, v, ACT.Gelu).then_inc(v_gelu.h, 1)

                for p in range(8):
                    u = UNIT["A"] + 2 * p
                    unit_is_done(0, u)
                    if p >= 2:
                        act.wait_ge(dve_evac.h, dve_evac.at(layer, DVE_EVAC["A"] + p - 1))
                    A(tile(atmp, p % 2), bank(u % 4), ACT.Sigmoid, bias=c1(col, COL["b_in"] + BT["ag"] + p)).then_inc(act_evac.h, 1)
                    weight_hi(0, u + 4, layer)
                    weight_hi(0, u + 5, layer)
                    if p == 0:
                        act.wait_ge(vstat_ready.h, vstat_ready.at(layer, 4))
                        A(vstd[:, :].rearrange("p (t a) -> p t a", a=1), vmv[:, :].rearrange("p (t a) -> p t a", a=2)[:, :, 1:2], ACT.Sqrt, bias=eps).then_inc(std_ready.h, 1)

                for g in range(8):
                    u = UNIT["U"] + g
                    unit_is_done(0, u)
                    if g < 2:
                        act.wait_ge(dve_evac.h, dve_evac.at(layer, DVE_EVAC["A"] + 7 + g))
                    else:
                        act.wait_ge(val_ready.h, val_ready.at(layer, SPLIT["U"] + g - 1))
                    A(tile(atmp, g % 2), bank(u % 4), ACT.Gelu, bias=c1(col, COL["b_in"] + BT["u"] + g)).then_inc(act_evac.h, 1)
                    weight_hi(0, u + 4, layer)
                    split_hi(mid_hi, OPA[0] + g, "U", g)

                def gate(branch, stage, n, b=None):
                    A(tile(atmp, n % 2), bank((UNIT[stage] + 2 * n) % 4 if b is None else b), ACT.Sigmoid,
                      bias=c1(col, COL["b_in"] + BT["gate"] + 8 * branch + n)).then_inc(act_evac.h, 1)

                for n in range(8):
                    u = UNIT["BRA"] + 2 * n
                    unit_is_done(0, u)
                    if n < 2:
                        act.wait_ge(val_ready.h, val_ready.at(layer, SPLIT["U"] + 7 + n))
                    else:
                        act.wait_ge(dve_evac.h, dve_evac.at(layer, DVE_EVAC["BRA"] + n - 1))
                    gate(0, "BRA", n)
                    weight_hi(0, u + 4, layer)
                    weight_hi(0, u + 5, layer)

                for k in range(8):
                    u = UNIT["P"] + k
                    unit_is_done(0, u)
                    if k >= 2:
                        act.wait_ge(val_ready.h, val_ready.at(layer, SPLIT["P"] + k - 1))
                    A(ptmp[:, k % 2 * PW + WMAX - 1:(k % 2 + 1) * PW], bank(u % 4), ACT.Identity,
                      bias=c1(col, COL["b_in"] + BT["p"] + k)).then_inc(act_evac.h, 1)
                    weight_hi(0, u + 4, layer)
                    split_hi(mid_hi, OPB[0] + k, "P", k)

                for q in range(2):
                    if q == 0:
                        weight_hi(0, UNIT["POOL"] + 4, layer)
                    for k in range(4 * q, 4 * q + 4):
                        split_hi(mid_hi, OPB[0] + k, "POOL", k)
                weight_hi(0, UNIT["POOL"] + 5, layer)

                for n in range(8):
                    u = UNIT["BRB"] + 2 * n
                    if n == 6:
                        act.wait_ge(stat_ready.h, stat_ready.at(layer, 3))
                        A(rstd[:, :], bank(6), ACT.Sqrt, bias=eps).then_inc(std_ready.h, 1)
                        for k in range(CT):
                            if k == 2:
                                weight_hi(0, u + 4, layer)
                            act.wait_ge(val_ready.h, val_ready.at(layer, SPLIT["C"] + k + 1))
                            if k >= 2:
                                act.wait_ge(x_lo.h, x_lo.at(layer, SPLIT["C"] + k - 1))
                            A(tile(sq, k % 2), tile(dtmp, k % 2), ACT.Silu, bias=c1(col, COL["conv_lb"] + k)).then_inc(silu_ready.h, 1)
                            act.wait_ge(silu_ready.h, silu_ready.at(layer, k + 1))
                            nc.scalar.copy(tile(mid_hi, OPA[0] + k), tile(sq, k % 2)).then_inc(x_hi.h, 1)
                        weight_hi(0, u + 5, layer)
                    unit_is_done(0, u)
                    if n < 2:
                        act.wait_ge(dve_evac.h, dve_evac.at(layer, DVE_EVAC["BRA"] + 7 + n))
                    else:
                        act.wait_ge(added.h, added.at(layer, n - 1))
                    gate(1, "BRB", n)
                    if n != 6:
                        weight_hi(0, u + 4, layer)
                        weight_hi(0, u + 5, layer)
                    if n == 4:
                        for k in range(CT):
                            act.wait_ge(centered.h, centered.at(layer, k + 1))
                            square(zc[:, k * ZW + PAD:(k + 1) * ZW], "C", k)

                for n in range(8):
                    u = UNIT["BRC"] + 2 * n
                    unit_is_done(0, u)
                    if n < 2:
                        act.wait_ge(added.h, added.at(layer, 7 + n))
                    else:
                        act.wait_ge(val_ready.h, val_ready.at(layer, SPLIT["BRC"] + n - 1))
                    gate(2, "BRC", n, None if n else BRC_BANK)
                    weight_hi(0, u + 4, layer)
                    split_hi(mid_hi, OPB[0] + n, "BRC", n)
                    weight_hi(0, u + 5, layer)

                for n in range(4):
                    weight_hi(0, UNIT["OUT"] + n + 4, layer)
                    act.wait_ge(dve_evac.h, dve_evac.at(layer, DVE_EVAC["OUT"] + n + 1))
                    square(tile(x, n), "OUT", n)

                def square_half(stage, e, n, f):
                    act.wait_ge(dve_evac.h, dve_evac.at(layer, DVE_EVAC[stage] + e + 1))
                    square(half(x, n, f), stage, e, f)

                for n in range(4, 8):
                    square_half("OUT", n, n, 0)
                std(layer, 4, 0)
                for k in range(CT):
                    if k in (0, 2, 6):
                        weight_hi(0, UNIT["FI"] + (0, 2, 6).index(k), layer)
                    act.wait_ge(val_ready.h, val_ready.at(layer, SPLIT["N2"] + k + 1))
                    A(half(h_hi, k, 0), tile(dtmp, k % 4, HS), ACT.Identity, bias=c1(ada, SH_F + k)).then_inc(x_hi.h, 1)
                for n in range(4, 8):
                    square_half("OUT", 4 + n, n, 1)
                weight_hi(0, UNIT["FI"] + 3, layer)
                std(layer, 5, 1)
                norm_half(1, SH_F, "N2")

                with act.Fori(0, FT // 2) as i:
                    for k in range(2):
                        c = UNIT["FI"] + 2 * k
                        unit_is_done(i, c)
                        act.wait_ge(val_ready.h, val_ready.at(layer, i * 2 + (SPLIT["FI"] + k - 1)))
                        A(tile(atmp, k), bank(c % 4), ACT.Silu).then_inc(act_evac.h, 1)
                        weight_hi(i, c + 4, layer)
                        act.wait_ge(val_ready.h, val_ready.at(layer, i * 2 + (SPLIT["FI"] + k + 1)))
                        nc.scalar.copy(mid_hi[:, ds((i * 2 + k) * S, S)], tile(dtmp, k)).then_inc(x_hi.h, 1)
                        weight_hi(i, c + 5, layer)

                for c in range(146, 148):
                    weight_hi(0, c, layer)
                with act.Fori(0, 4) as i:
                    for c in range(4):
                        weight_hi(i, 148 + c, layer)
                for e in range(8):
                    square_half("FO", e, e, 0)
                std(layer, 6, 0)
                for e, n in enumerate(FO_B):
                    square_half("FO", 8 + e, n, 1)
                    if e == 0:
                        weight_hi(0, UNITS, layer)
                        weight_hi(0, UNITS + 1, layer)

            std(DEPTH, 1, 1)


        @block.vector
        def _(dve):
            V = nc.vector
            steps = Steps(dve, dve_step)

            def did(ins):
                steps.did(ins)

            def then(ins):
                steps.did(ins)
                steps.settle()

            def add_square(layer, stage, e, f=None, first=False):
                n = SQ[stage] + e
                dve.wait_ge(sq_ready.h, sq_ready.at(layer, n + 1))
                total, square = (ssum[:, :], tile(sq, e % 2)) if f is None else (half(ssum, 0, f), half(sq, e % 2, f))
                if first:
                    V.tensor_copy(total, square).then_inc(sq_added.h, 1)
                else:
                    dve.wait_ge(sq_added.h, sq_added.at(layer, n))
                    V.tensor_tensor(total, total, square, ALU.add).then_inc(sq_added.h, 1)

            def ada_finish(scratch, layer, n, at_col, bias_at, settle=True, b=4):
                dve.wait_ge(ada_ready.h, ada_ready.at(layer, n + 1))
                r3 = scratch.rearrange("p (c n) -> p c n", c=4)
                V.tensor_tensor(r3, bank(b).rearrange("p (c n) -> p c n", c=4),
                                ident.rearrange("p (a n) -> p a n", a=1).to_broadcast([P, 4, P]), ALU.mult).then_inc(ada_read.h, 1)
                dve.wait_ge(ada_read.h, ada_read.at(layer, n + 1))
                then(V.reduce_sum(ada[:, ds(at_col, 4)], r3, AX.X))
                did(V.tensor_tensor(ada[:, ds(at_col, 4)], ada[:, ds(at_col, 4)], fix[:, ds(bias_at, 4)], ALU.add))
                if settle:
                    steps.settle()

            dve.wait_ge(fix_in.h, 16)
            dve.sem_inc(ada_used.h, 2)
            dve.wait_ge(c_ready.h, 1)
            for h in range(4):
                acc = tile(pro_acc, h)
                for k in range(PRO_DVE):
                    if h == 3 and k % 2 == 0:
                        dve.wait_ge(pro_in[3 + k // 2].h, 16)
                    elif k == 0:
                        dve.wait_ge(pro_in[h].h, 16)
                    w = tile(pro_raw[h], k)
                    if k == 0:
                        then(V.tensor_scalar(acc, w, c1(cact, k), None, ALU.mult))
                    elif k < PRO_DVE - 1:
                        then(V.scalar_tensor_tensor(out=acc, in0=w, scalar=c1(cact, k), in1=acc, op0=ALU.mult, op1=ALU.add))
                    else:
                        V.scalar_tensor_tensor(out=acc, in0=w, scalar=c1(cact, k), in1=acc,
                                               op0=ALU.mult, op1=ALU.add).then_inc(pro_acc_ready.h, 1)
                if h == 3:
                    dve.wait_ge(std_ready.h, std_ready.at(0, 0))
                    then(V.reciprocal(half(rstd, 0, 0), half(rstd, 0, 0)))
                if h:
                    ada_finish(tile(atmp, 0), 0, h - 1 - 4, SH_M + 4 * (h - 1), FIX["b_ada"] + 4 * (h - 1), b=4 + (h - 1) % 2)
            ada_finish(tile(atmp, 0), 0, -1, SH_M + 12, FIX["b_ada"] + 12, b=5)
            dve_step.start = steps.n
            steps.n = 0

            with dve.Fori(0, DEPTH) as layer:
                steps.layer = layer

                def unit_is_done(i, c):
                    dve.wait_ge(unit_done.h, unit_done.at(layer, i * 4 + (c + 1)))

                def split_lo(val, hi, lo, stage, k):
                    dve.wait_ge(x_hi.h, x_hi.at(layer, SPLIT[stage] + k + 1))
                    V.tensor_tensor(lo, val, hi.bitcast(f32), ALU.subtract).then_inc(x_lo.h, 1)

                def slot_is_split(stage, k):
                    if SPLIT[stage] + k >= 2:
                        dve.wait_ge(x_lo.h, x_lo.at(layer, SPLIT[stage] + k - 1))

                def ada_chunk(i, k, m):
                    dve.wait_ge(ada_in[k % 2].h, ada_in[k % 2].at(layer, i * (m // 2) + (k // 2 + 1)))
                    w0, w1 = (ada_raw[:, k % 2 * UC + 512 * j:k % 2 * UC + 512 * (j + 1)] for j in range(2))
                    kt = 2 * (k % 4)
                    if k % 4 == 0:
                        then(V.tensor_scalar(ada_acc[:, :], w0, c1(cact, kt), None, ALU.mult))
                    else:
                        dve.wait_ge(ada_used.h, ada_used.at(layer, i * m + k))
                        then(V.scalar_tensor_tensor(out=ada_acc[:, :], in0=w0, scalar=c1(cact, kt), in1=ada_acc[:, :],
                                                    op0=ALU.mult, op1=ALU.add))
                    V.scalar_tensor_tensor(out=ada_acc[:, :], in0=w1, scalar=c1(cact, kt + 1), in1=ada_acc[:, :],
                                           op0=ALU.mult, op1=ALU.add).then_inc(ada_used.h, 1)

                def finish(n, settle=True, scratch=rstd[:, :]):
                    ada_finish(scratch, layer, n, 4 * n, layer * 48 + (FIX["b_ada"] + 16 + 4 * n), settle)

                def gains(g, scale):
                    then(V.tensor_scalar(gain[:, :], ada[:, scale:scale + CT], 1.0, None, ALU.add))
                    then(V.tensor_tensor(gain[:, :], gain[:, :], g, ALU.mult))

                def norm_half(f, shift, stage, between=None):
                    for k in range(CT + 2):
                        if k < CT:
                            e = SPLIT[stage] + f * CT + k
                            if e >= 4:
                                dve.wait_ge(x_lo.h, x_lo.at(layer, e - 3))
                            V.scalar_tensor_tensor(out=tile(dtmp, k % 4, HS), in0=half(x, k, f), scalar=c1(gain, k),
                                                   in1=half(rstd, 0, f), op0=ALU.mult, op1=ALU.mult).then_inc(val_ready.h, 1)
                        if k >= 2:
                            dve.wait_ge(x_hi.h, x_hi.at(layer, SPLIT[stage] + f * CT + k - 1))
                            V.scalar_tensor_tensor(out=half(h_lo, k - 2, f), in0=tile(dtmp, (k - 2) % 4, HS),
                                                   scalar=c1(ada, shift + k - 2), in1=half(h_hi, k - 2, f).bitcast(f32),
                                                   op0=ALU.add, op1=ALU.subtract).then_inc(x_lo.h, 1)
                        if between and k < CT:
                            between(k)

                def half_reciprocal(layer_, n_std, f):
                    dve.wait_ge(std_ready.h, std_ready.at(layer_, n_std))
                    then(V.reciprocal(half(rstd, 0, f), half(rstd, 0, f)))

                def half_update(psum_half, n, f, gate):
                    V.scalar_tensor_tensor(out=half(x, n, f), in0=psum_half, scalar=c1(ada, gate + n), in1=half(x, n, f),
                                           op0=ALU.mult, op1=ALU.add).then_inc(dve_evac.h, 1)

                def conv_taps(first, last):
                    for n in range(first, last):
                        j, k = divmod(n, TAPS)
                        z = zc[:, j * ZW + k:j * ZW + k + S]
                        w = c1(col, COL["conv_w"] + j * TAPS + k)
                        if k == 0:
                            then(V.tensor_scalar(bank(7), z, w, c1(col, COL["conv_b"] + j), ALU.mult, ALU.add))
                        elif k < TAPS - 1:
                            then(V.scalar_tensor_tensor(out=bank(7), in0=z, scalar=w, in1=bank(7), op0=ALU.mult, op1=ALU.add))
                        else:
                            then(V.scalar_tensor_tensor(out=z, in0=z, scalar=w, in1=bank(7), op0=ALU.mult, op1=ALU.add))
                            if j == 1:
                                did(V.tensor_tensor(ssum[:, :], zc[:, PAD:ZW], z, ALU.add))
                            elif 1 < j < CT - 1:
                                did(V.tensor_tensor(ssum[:, :], ssum[:, :], z, ALU.add))
                            elif j == CT - 1:
                                V.tensor_tensor(ssum[:, :], ssum[:, :], z, ALU.add).then_inc(zsum_ready.h, 1)

                dve.wait_ge(col_in.h, col_in.at(layer, 1))
                gains(col[:, COL["g_mix"]:COL["g_mix"] + CT], SC_M)
                norm_half(0, SH_M, "N1")
                half_reciprocal(layer, 1, 1)
                norm_half(1, SH_M, "N1")
                z3 = zc[:, :].rearrange("p (j t) -> p j t", j=CT)
                dve.wait_ge(layer_in.h, layer_in.at(layer, 5))
                for h in range(2):
                    unit_is_done(0, 4 * h + 3)
                    for tt in range(4):
                        V.tensor_tensor(vtok[:, tt * D + h * 512:tt * D + h * 512 + 512], bank(4 * h + tt),
                                        bc[:, h * 512:h * 512 + 512], ALU.add).then_inc(dve_evac.h, 1)
                for tt in range(4):
                    for h in range(2):
                        dve.wait_ge(v_gelu.h, v_gelu.at(layer, 4 * h + tt + 1))
                        did(V.bn_stats(vbn[:, (2 * tt + h) * 6:(2 * tt + h + 1) * 6],
                                       vtok[:, tt * D + h * 512:tt * D + h * 512 + 512]))
                steps.settle()
                did(V.memset(z3[:, :, 0:PAD], 0.0))
                for tt in range(4):
                    V.bn_aggr(vmv[:, 2 * tt:2 * tt + 2], vbn[:, 12 * tt:12 * tt + 12]).then_inc(vstat_ready.h, 1)

                for p in range(8):
                    u = UNIT["A"] + 2 * p
                    dve.wait_ge(act_evac.h, act_evac.at(layer, ACT_EVAC["A"] + p + 1))
                    unit_is_done(0, u + 1)
                    V.scalar_tensor_tensor(out=z3[:, p, PAD:ZW], in0=bank((u + 1) % 4), scalar=c1(col, COL["b_in"] + BT["a"] + p),
                                           in1=tile(atmp, p % 2), op0=ALU.add, op1=ALU.mult).then_inc(dve_evac.h, 1)
                    if p == 1:
                        dve.wait_ge(std_ready.h, std_ready.at(layer, 2))
                        then(V.reciprocal(vstd[:, :], vstd[:, :]))
                    if 1 <= p <= 4:
                        for tt in (p - 1,):
                            v = vtok[:, tt * D:(tt + 1) * D]
                            then(V.tensor_scalar(v, v, c1(vmv, 2 * tt), c1(vstd, tt), ALU.subtract, ALU.mult))
                            then(V.tensor_tensor(v, v, bc[:, D:2 * D], ALU.mult))
                            V.tensor_tensor(v, v, bc[:, 2 * D:3 * D], ALU.add).then_inc(v_ready.h, 1)
                    dve.wait_ge(dve_evac.h, dve_evac.at(layer, DVE_EVAC["A"] + p + 1))
                    conv_taps(*A_TAPS[p:p + 2])

                for g in range(8):
                    dve.wait_ge(mixed_ready.h, mixed_ready.at(layer, g + 1))
                    b_s = bc[:, 3 * D + g * P:3 * D + (g + 1) * P].rearrange("p (a t) -> p a t", a=1).to_broadcast([P, 4, P])
                    V.tensor_tensor(tile(sq, g % 2).rearrange("p (n t) -> p n t", n=4),
                                    bank(4 + g % 2).rearrange("p (n t) -> p n t", n=4), b_s, ALU.add).then_inc(dve_evac.h, 1)
                    dve.wait_ge(act_evac.h, act_evac.at(layer, ACT_EVAC["U"] + g + 1))
                    dve.wait_ge(dve_evac.h, dve_evac.at(layer, DVE_EVAC["U"] + g + 1))
                    slot_is_split("U", g)
                    V.tensor_tensor(tile(dtmp, g % 2), tile(sq, g % 2), tile(atmp, g % 2), ALU.mult).then_inc(val_ready.h, 1)
                    conv_taps(U_TAPS + 5 * g, U_TAPS + 5 * (g + 1))
                    split_lo(tile(dtmp, g % 2), tile(mid_hi, OPA[0] + g), tile(mid_lo, OPA[1] + g), "U", g)

                for n in range(8):
                    u = UNIT["BRA"] + 2 * n
                    dve.wait_ge(act_evac.h, act_evac.at(layer, ACT_EVAC["BRA"] + n + 1))
                    unit_is_done(0, u + 1)
                    V.tensor_tensor(tile(merged, n), bank((u + 1) % 4), tile(atmp, n % 2), ALU.mult).then_inc(dve_evac.h, 1)
                    conv_taps(*BRA_TAPS[n:n + 2])

                then(V.memset(ptmp[:, :].rearrange("p (a t) -> p a t", a=2)[:, :, 0:WMAX - 1], 0.0))
                for k in range(8):
                    win = WINDOWS[k // 2]
                    src = ptmp[:, k % 2 * PW:(k % 2 + 1) * PW]
                    dve.wait_ge(act_evac.h, act_evac.at(layer, ACT_EVAC["P"] + k + 1))
                    have, span, b = src, 1, 0
                    while span < win:
                        span *= 2
                        lo = WMAX - 1 - (win - span)
                        nxt = wsum[:, b * PW:(b + 1) * PW]
                        then(V.tensor_tensor(nxt[:, lo:PW], have[:, lo:PW], have[:, lo - span // 2:PW - span // 2], ALU.add))
                        have, b = nxt, 1 - b
                    head = have[:, WMAX - 1:WMAX - 1 + WMAX]
                    hd = FIX["head"] + k // 2 * WMAX
                    then(V.tensor_tensor(head, head, fix[:, hd:hd + WMAX], ALU.mult))
                    slot_is_split("P", k)
                    V.scalar_tensor_tensor(out=tile(dtmp, k % 2), in0=have[:, WMAX - 1:PW], scalar=1.0 / win,
                                           in1=src[:, WMAX - 1:PW], op0=ALU.mult, op1=ALU.subtract).then_inc(val_ready.h, 1)
                    conv_taps(*P_TAPS[k:k + 2])
                    split_lo(tile(dtmp, k % 2), tile(mid_hi, OPB[0] + k), tile(mid_lo, OPB[1] + k), "P", k)

                for k in range(8):
                    unit_is_done(0, UNIT["POOL"] + k // 4)
                    if k >= 2:
                        split_lo(tile(dtmp, k % 2), tile(mid_hi, OPB[0] + k - 2), tile(mid_lo, OPB[1] + k - 2), "POOL", k - 2)
                    slot_is_split("POOL", k)
                    V.tensor_scalar(tile(dtmp, k % 2), bank(k % 7), c1(col, COL["pool_scale"] + k), None,
                                    ALU.mult).then_inc(val_ready.h, 1)
                for k in (6, 7):
                    split_lo(tile(dtmp, k % 2), tile(mid_hi, OPB[0] + k), tile(mid_lo, OPB[1] + k), "POOL", k)

                for n in range(8):
                    def branch_b():
                        u = UNIT["BRB"] + 2 * n
                        dve.wait_ge(act_evac.h, act_evac.at(layer, ACT_EVAC["BRB"] + n + 1))
                        unit_is_done(0, u + 1)
                        V.tensor_tensor(tile(atmp, n % 2), bank((u + 1) % 4), tile(atmp, n % 2), ALU.mult).then_inc(dve_evac.h, 1)
                        dve.wait_ge(dve_evac.h, dve_evac.at(layer, DVE_EVAC["BRB"] + n + 1))
                        V.tensor_tensor(tile(merged, n), tile(merged, n), tile(atmp, n % 2), ALU.add).then_inc(added.h, 1)

                    if n == 6:
                        dve.wait_ge(std_ready.h, std_ready.at(layer, 3))
                        then(V.reciprocal(rstd[:, :], rstd[:, :]))
                        for k in range(CT + 2):
                            if k >= 2:
                                split_lo(tile(sq, k % 2), tile(mid_hi, OPA[0] + k - 2), tile(mid_lo, OPA[1] + k - 2), "C", k - 2)
                            if k < CT:
                                V.scalar_tensor_tensor(out=tile(dtmp, k % 2), in0=z3[:, k, PAD:ZW], scalar=c1(col, COL["conv_g"] + k),
                                                       in1=rstd[:, :], op0=ALU.mult, op1=ALU.mult).then_inc(val_ready.h, 1)
                        for c in (6, 7):
                            ada_chunk(0, c, 8)
                    branch_b()
                    if n < 4:
                        ada_chunk(0, n, 8)
                        conv_taps(*BRB_TAPS[n:n + 2])
                    if n == 4:
                        dve.wait_ge(stat_ready.h, stat_ready.at(layer, 2))
                        for k in range(CT + 2):
                            if k < CT:
                                V.tensor_tensor(z3[:, k, PAD:ZW], z3[:, k, PAD:ZW], bank(6), ALU.subtract).then_inc(centered.h, 1)
                            if k >= 2:
                                add_square(layer, "C", k - 2, first=k == 2)
                        finish(0, scratch=tile(dtmp, 0))
                        ada_chunk(0, 4, 8)
                    if n == 5:
                        ada_chunk(0, 5, 8)

                for n in range(8):
                    u = UNIT["BRC"] + 2 * n
                    if n % 2 == 0:
                        finish(1 + n // 2)
                    ada_chunk(0, 8 + 2 * n, 48)
                    if n % 2:
                        ada_chunk(0, 9 + 2 * n, 48)
                    dve.wait_ge(act_evac.h, act_evac.at(layer, ACT_EVAC["BRC"] + n + 1))
                    unit_is_done(0, u + 1)
                    V.tensor_tensor(tile(atmp, n % 2), bank((u + 1) % 4), tile(atmp, n % 2), ALU.mult).then_inc(dve_evac.h, 1)
                    dve.wait_ge(dve_evac.h, dve_evac.at(layer, DVE_EVAC["BRC"] + n + 1))
                    slot_is_split("BRC", n)
                    V.tensor_tensor(tile(dtmp, n % 2), tile(merged, n), tile(atmp, n % 2), ALU.add).then_inc(val_ready.h, 1)
                    split_lo(tile(dtmp, n % 2), tile(mid_hi, OPB[0] + n), tile(mid_lo, OPB[1] + n), "BRC", n)
                    if n % 2 == 0:
                        ada_chunk(0, 9 + 2 * n, 48)

                finish(5)
                for n in range(4):
                    u = UNIT["OUT"] + n
                    unit_is_done(0, u)
                    V.scalar_tensor_tensor(out=tile(x, n), in0=bank(u % 4), scalar=c1(ada, GT_M + n), in1=tile(x, n),
                                           op0=ALU.mult, op1=ALU.add).then_inc(dve_evac.h, 1)
                    if n == 3:
                        finish(6)
                    for k in ((24, 25), (26, 27), (), (28, 29))[n]:
                        ada_chunk(0, k, 48)
                    add_square(layer, "OUT", n, first=n == 0)
                for n in range(4, 8):
                    u = UNIT["OUT"] + n
                    dve.wait_ge(out_half.h, out_half.at(layer, n - 3))
                    half_update(half(bank(u % 4), 0, 0), n, 0, GT_M)
                    if n == 4:
                        gains(col[:, COL["g_ffn"]:COL["g_ffn"] + CT], SC_F)
                    add_square(layer, "OUT", n, 0)

                half_reciprocal(layer, 4, 0)

                def rest_of_x(k):
                    if k % 2:
                        n = 4 + k // 2
                        unit_is_done(0, UNIT["OUT"] + n)
                        half_update(half(bank((UNIT["OUT"] + n) % 4), 0, 1), n, 1, GT_M)

                norm_half(0, SH_F, "N2", rest_of_x)
                for n in range(4, 8):
                    add_square(layer, "OUT", 4 + n, 1)
                half_reciprocal(layer, 5, 1)
                norm_half(1, SH_F, "N2")
                for k in (30, 31):
                    ada_chunk(0, k, 48)

                def ffn_pair(i, k, m):
                    c = UNIT["FI"] + 2 * k
                    dve.wait_ge(act_evac.h, act_evac.at(layer, i * m + (ACT_EVAC["FI"] + k + 1)))
                    dve.wait_ge(unit_done.h, unit_done.at(layer, i * (2 * m) + (c + 2)))
                    dve.wait_ge(x_lo.h, x_lo.at(layer, i * m + (SPLIT["FI"] + k - 1)))
                    V.tensor_tensor(tile(dtmp, k % 2), bank((c + 1) % 4), tile(atmp, k % 2), ALU.mult).then_inc(val_ready.h, 1)
                    dve.wait_ge(x_hi.h, x_hi.at(layer, i * m + (SPLIT["FI"] + k + 1)))
                    V.tensor_tensor(mid_lo[:, ds((i * m + k) * S, S)], tile(dtmp, k % 2),
                                    mid_hi[:, ds((i * m + k) * S, S)].bitcast(f32), ALU.subtract).then_inc(x_lo.h, 1)

                with dve.Fori(0, 4) as i:
                    steps.loop, inside = i * 6, steps.n
                    for k in range(4):
                        ffn_pair(i, k, 4)
                        if k == 0:
                            n = 7
                            ada_finish(rstd[:, :], layer, i + n, i * 4 + 4 * n, layer * 48 + (i * 4 + (FIX["b_ada"] + 16 + 4 * n)))
                        ada_chunk(i, 32 + k, 4)
                    assert steps.n - inside == 6
                    steps.loop, steps.n = None, inside + 4 * 6
                for k in range(2):
                    ffn_pair(0, 16 + k, 2)
                finish(11, settle=False)
                with dve.Fori(0, 2) as i:
                    for k in range(2):
                        ffn_pair(i, 18 + k, 2)

                steps.settle()
                for e in range(16):
                    f, n = (0, e) if e < 8 else (1, FO_B[e - 8])
                    if e < 15:
                        dve.wait_ge(ff_bank.h, ff_bank.at(layer, e + 1))
                    else:
                        unit_is_done(0, UNITS - 1)
                    half_update(half(bank(n), 0, f), n, f, GT_F)
                    if e == 8:
                        half_reciprocal(layer, 6, 0)
                assert steps.n == DVE_STEPS, steps.n

            for f in range(2):
                if f:
                    dve.wait_ge(std_ready.h, std_ready.at(DEPTH, 1))
                    V.reciprocal(half(rstd, 0, 1), half(rstd, 0, 1)).then_inc(last_std.h, 1)
                    dve.wait_ge(last_std.h, 1)
                for k in range(CT):
                    V.scalar_tensor_tensor(out=half(x, k, f), in0=half(x, k, f), scalar=c1(fix, FIX["g_final"] + k),
                                           in1=half(rstd, 0, f), op0=ALU.mult, op1=ALU.mult).then_inc(y_ready.h, 1)

        @block.tensor
        def _(pe):
            pe.sem_inc(unit_done.h, RING)
            pe.wait_ge(fix_in.h, 16)

            def ada_sum(layer, n, acc):
                pe.wait_ge(ada_read.h, ada_read.at(layer, n))
                pe.matmul(bank(4), ones, acc, start=True, stop=True).then_inc(ada_ready.h, 1)

            def half_sum(layer, n_sq, f, n_std=None):
                pe.wait_ge(sq_added.h, sq_added.at(layer, n_sq))
                if n_std is not None:
                    pe.wait_ge(std_ready.h, std_ready.at(layer, n_std))
                pe.matmul(half(bank(6), 0, f), mean, half(ssum, 0, f), start=True, stop=True).then_inc(stat_ready.h, 1)

            pe.wait_ge(c_ready.h, 1)
            for h in range(4):
                if h >= 2:
                    pe.wait_ge(ada_read.h, ada_read.at(0, h - 1 - 4))
                pe.wait_ge(pro_in[h if h < 3 else 6].h, 16)
                for k in range(PRO_DVE, CT):
                    pe.matmul(bank(4 + h % 2), c1(cact, k).to_broadcast([P, P]), tile(pro_raw[h], k), start=(k == PRO_DVE), stop=False)
                pe.wait_ge(pro_acc_ready.h, h + 1)
                pe.matmul(bank(4 + h % 2), ones, tile(pro_acc, h), start=False, stop=True).then_inc(ada_ready.h, 1)
                if h == 2:
                    half_sum(0, 0, 0)

            with pe.Fori(0, DEPTH) as layer:
                def unit_is_split(i, c):
                    pe.wait_ge(w_lo_done.h, w_lo_done.at(layer, i * 4 + (c + 1)))

                def passes(hi, lo, whi_, wlo_, stationary):
                    for a, b in ((hi, whi_), (lo, whi_), (hi, wlo_)):
                        yield (a, b) if stationary else (b, a)

                def unit(i, c, operand, free=None, tiles=None, f=None, kts=range(8), b=None):
                    s = c % RING
                    if free:
                        pe.wait_ge(free[0].h, free[0].at(layer, free[1]))
                    if not f and kts[0] == 0:
                        unit_is_split(i, c)
                    hi, lo, th, tl = operand
                    part = tile if f is None else (lambda t, k: half(t, k, f))
                    for kt in kts:
                        if tiles:
                            pe.wait_ge(x_lo.h, x_lo.at(layer, tiles + kt + 1))
                        w = slice(s * UC + kt * P, s * UC + (kt + 1) * P)
                        for j, (st, mv) in enumerate(passes(part(hi, th + kt), part(lo, tl + kt), whi[:, w], wlo[:, w], False)):
                            mm = pe.matmul(part(bank(s if b is None else b), 0), st, mv, start=(kt == 0 and j == 0), stop=(kt == 7 and j == 2))
                    if f != 0:
                        mm.then_inc(unit_done.h, 1)
                    return mm

                H = (h_hi, h_lo, 0, 0)
                opa = (mid_hi, mid_lo, *OPA)
                opb = (mid_hi, mid_lo, *OPB)

                def channel_sum(wait, n):
                    pe.wait_ge(wait.h, n)
                    pe.matmul(bank(6), mean, ssum[:, :], start=True, stop=True).then_inc(stat_ready.h, 1)

                def v_unit(h, q, tts, ready=None):
                    for j in range(2):
                        kt = 2 * q + j
                        if ready is not None:
                            pe.wait_ge(x_lo.h, x_lo.at(layer, SPLIT["N1"] + ready + kt + 1))
                        w = slice(q * UC + j * 512, q * UC + (j + 1) * 512)
                        for tt in tts:
                            t = slice(kt * S + tt * P, kt * S + (tt + 1) * P)
                            for m, (st, mv) in enumerate(passes(h_hi[:, t], h_lo[:, t], whi[:, w], wlo[:, w], True)):
                                mm = pe.matmul(bank(4 * h + tt), st, mv, start=(kt == 0 and m == 0), stop=(kt == 7 and m == 2))
                    return mm

                for q in range(4):
                    unit_is_split(0, q)
                    v_unit(0, q, (0, 1), 0)
                    if q == 0:
                        half_sum(layer, 0, 1, 0)
                for q in range(4):
                    v_unit(0, q, (2, 3), CT).then_inc(unit_done.h, 1)
                for q in range(4):
                    unit_is_split(0, 4 + q)
                    v_unit(1, q, range(4)).then_inc(unit_done.h, 1)

                for c in range(4):
                    unit(0, UNIT["A"] + c, H, free=(dve_evac, DVE_EVAC["V"] + c + 1))
                with pe.Fori(0, 3) as i:
                    for c in range(4):
                        f = (act_evac, i * 2 + (ACT_EVAC["A"] + c // 2 + 1)) if c % 2 == 0 else (dve_evac, i * 2 + (DVE_EVAC["A"] + c // 2 + 1))
                        unit(i, UNIT["A"] + 4 + c, H, free=f)

                pe.wait_ge(ws_masked.h, ws_masked.at(layer, 1))
                for g in range(8):
                    if g == 0:
                        pe.wait_ge(v_ready.h, v_ready.at(layer, 4))
                    pe.wait_ge(dve_evac.h, dve_evac.at(layer, DVE_EVAC["V"] + 5 + g if g < 2 else DVE_EVAC["U"] + g - 1))
                    for tt in range(4):
                        mm = pe.matmul(psum[:, (4 + g % 2) * 512 + tt * P:(4 + g % 2) * 512 + (tt + 1) * P],
                                       vtok[:, tt * D + g * P:tt * D + (g + 1) * P], wsT[:, g * P:(g + 1) * P], start=True, stop=True)
                    mm.then_inc(mixed_ready.h, 1)
                    if g < 4:
                        f = (act_evac, ACT_EVAC["A"] + 7 + g // 2) if g % 2 == 0 else (dve_evac, DVE_EVAC["A"] + 7 + g // 2)
                    else:
                        f = (act_evac, ACT_EVAC["U"] + g - 3)
                    unit(0, UNIT["U"] + g, H, free=f)

                def branch(stage, body, operand, ready, prev=None, behind={}):
                    i, k = body
                    for c in range(4):
                        if prev:
                            f = prev[c]
                        elif c % 2 == 0:
                            f = (act_evac, i * 2 + (ACT_EVAC[stage] + 2 * (k - 1) + c // 2 + 1))
                        else:
                            f = (dve_evac, i * 2 + (DVE_EVAC[stage] + 2 * (k - 1) + c // 2 + 1))
                        first = k == 0 and c == 1
                        own = BRC_BANK if stage == "BRC" and k == 0 and c == 0 else None
                        unit(i, UNIT[stage] + 4 * k + c, H if c % 2 == 0 else operand, free=f, tiles=ready if first else None, b=own)
                        if c in behind:
                            behind[c]()

                branch("BRA", (0, 0), opa, SPLIT["U"], [(act_evac, ACT_EVAC["U"] + 5 + c) for c in range(4)])
                with pe.Fori(0, 3) as i:
                    branch("BRA", (i, 1), opa, SPLIT["U"])

                for c in range(4):
                    f = (act_evac, ACT_EVAC["BRA"] + 7 + c // 2) if c % 2 == 0 else (dve_evac, DVE_EVAC["BRA"] + 7 + c // 2)
                    unit(0, UNIT["P"] + c, H, free=f)
                for c in range(4):
                    unit(0, UNIT["P"] + 4 + c, H, free=(act_evac, ACT_EVAC["P"] + c + 1))

                for q in range(2):
                    c = UNIT["POOL"] + q
                    unit_is_split(0, c)
                    for g in (2 * q, 2 * q + 1):
                        pe.wait_ge(x_lo.h, x_lo.at(layer, SPLIT["P"] + 2 * g + 2))
                        for nt in range(2):
                            k = 2 * g + nt
                            if k < 4:
                                pe.wait_ge(act_evac.h, act_evac.at(layer, ACT_EVAC["P"] + 5 + k))
                            elif k < 6:
                                pe.wait_ge(dve_evac.h, dve_evac.at(layer, DVE_EVAC["U"] + 3 + k))
                            elif k == 7:
                                pe.wait_ge(val_ready.h, val_ready.at(layer, SPLIT["POOL"] + 1))
                            for kt in range(2):
                                o = (c % RING) * UC + (g % 2) * 512 + kt * 256 + nt * P
                                hi, lo = tile(mid_hi, OPB[0] + 2 * g + kt), tile(mid_lo, OPB[1] + 2 * g + kt)
                                for m, (st, mv) in enumerate(passes(hi, lo, whi[:, o:o + P], wlo[:, o:o + P], False)):
                                    mm = pe.matmul(bank(k % 7), st, mv, start=(kt == 0 and m == 0), stop=(kt == 1 and m == 2))
                    mm.then_inc(unit_done.h, 1)

                branch("BRB", (0, 0), opb, SPLIT["POOL"], [(val_ready, SPLIT["POOL"] + n) for n in (3, 4, 8, 2)])
                branch("BRB", (0, 1), opb, SPLIT["POOL"])

                def mean_sum():
                    channel_sum(zsum_ready, zsum_ready.at(layer, 1))

                def variance_sum():
                    channel_sum(sq_added, sq_added.at(layer, SQ["C"] + 8))

                def half_vector(n):
                    def f():
                        pe.wait_ge(ada_used.h, ada_used.at(layer, 4 * n + 4))
                        ada_sum(layer, n, ada_acc[:, :])
                    return f

                branch("BRB", (0, 2), opb, SPLIT["POOL"], behind={0: half_vector(0), 1: mean_sum, 3: variance_sum})
                branch("BRB", (0, 3), opb, SPLIT["POOL"])

                for k in range(4):
                    prev = None if k else [(val_ready, SPLIT["POOL"] + 6), (dve_evac, DVE_EVAC["BRB"] + 7),
                                           (act_evac, ACT_EVAC["BRB"] + 8), (dve_evac, DVE_EVAC["BRB"] + 8)]
                    branch("BRC", (0, k), opa, SPLIT["C"], prev, behind={0: half_vector(1 + k)})

                half_vector(5)()
                for c in range(4):
                    f = (act_evac, ACT_EVAC["BRC"] + 7 + c // 2) if c % 2 == 0 else (dve_evac, DVE_EVAC["BRC"] + 7 + c // 2)
                    unit(0, UNIT["OUT"] + c, opb, free=f, tiles=SPLIT["BRC"] if c == 0 else None)
                    if c == 2:
                        half_vector(6)()
                for c in range(4, 8):
                    unit(0, UNIT["OUT"] + c, opb, free=(dve_evac, DVE_EVAC["OUT"] + c - 3), f=0).then_inc(out_half.h, 1)
                for c in range(4, 8):
                    unit(0, UNIT["OUT"] + c, opb, free=(dve_evac, DVE_EVAC["OUT"] + c + 1), f=1)
                    if c == 4:
                        half_sum(layer, SQ["OUT"] + 8, 0)

                def ffn_units(i, m, k, behind=None):
                    for c in range(4):
                        if c % 2 == 0:
                            f = (act_evac, i * (2 * m) + (ACT_EVAC["FI"] + 2 * k - 1 + c // 2))
                        else:
                            f = (val_ready, i * (2 * m) + (SPLIT["FI"] + 2 * k - 1 + c // 2))
                        unit(i * m if m > 1 else i, UNIT["FI"] + 4 * k + c, H, free=f)
                        if behind and c == 0:
                            behind()

                for c in (0, 2):
                    for k0 in (0, 4):
                        for d in (c, c + 1):
                            unit(0, UNIT["FI"] + d, H, kts=range(k0, k0 + 4), tiles=SPLIT["N2"] if d == 0 else None, f=0,
                                 free=(dve_evac, DVE_EVAC["OUT"] + 9 + d) if k0 == 0 else None)
                    if c == 0:
                        half_sum(layer, SQ["OUT"] + 12, 1, 4)
                for c in range(4):
                    unit(0, UNIT["FI"] + c, H, tiles=SPLIT["N2"] + CT if c == 0 else None, f=1)
                half_vector(7)()
                ffn_units(0, 1, 1)
                with pe.Fori(0, 3) as i:
                    def next_half():
                        pe.wait_ge(ada_used.h, ada_used.at(layer, i * 4 + 36))
                        ada_sum(layer, i + 8, ada_acc[:, :])
                    ffn_units(i, 2, 2, next_half)
                    ffn_units(i, 2, 3)
                ffn_units(0, 1, 8, half_vector(11))
                with pe.Fori(0, 2) as i:
                    ffn_units(i, 1, 9)

                def ff_matmuls(kt, s, n, first, last, f=None):
                    w = slice(s * UC + n * P, s * UC + (n + 1) * P)
                    t = ds(kt * S, S) if f is None else slice(kt * S + f * HS, kt * S + (f + 1) * HS)
                    for m, (st, mv) in enumerate(passes(mid_hi[:, t], mid_lo[:, t], whi[:, w], wlo[:, w], False)):
                        mm = pe.matmul(bank(n) if f is None else half(bank(n), 0, f), st, mv, start=(first and m == 0), stop=(last and m == 2), skip_group_check=(f == 1))
                    return mm

                def ff_unit(i, k, first=False):
                    c = UNIT["FO"] + k
                    unit_is_split(i, c)
                    pe.wait_ge(x_lo.h, x_lo.at(layer, i * 4 + (SPLIT["FI"] + k + 1)))
                    for n in range(8):
                        if first and n < 4:
                            order = (n - UNIT["FO"]) % 4
                            e = (act_evac, ACT_EVAC["FI"] + FT - 1 + order // 2) if order % 2 == 0 else (val_ready, SPLIT["FI"] + FT - 1 + order // 2)
                            pe.wait_ge(e[0].h, e[0].at(layer, e[1]))
                        if first and n == 4:
                            pe.wait_ge(ada_read.h, ada_read.at(layer, 12))
                        mm = ff_matmuls(i * 4 + k, c % RING, n, first, False)
                    mm.then_inc(unit_done.h, 1)

                ff_unit(0, 0, first=True)
                ff_unit(0, 1)
                with pe.Fori(0, 4) as i:
                    for k in range(4):
                        ff_unit(i, 2 + k)
                pe.wait_ge(x_lo.h, x_lo.at(layer, SPLIT["FI"] + FT))
                def ff_half(n, ks, f):
                    for k in ks:
                        mm = ff_matmuls(FT - 4 + k, k, n, False, k == 3, f)
                    return mm

                for k in range(2):
                    unit_is_split(0, UNITS - 4 + k)
                    for n in range(8):
                        ff_half(n, (k,), 0)
                for k in (2, 3):
                    unit_is_split(0, UNITS - 4 + k)
                for n in range(8):
                    ff_half(n, (2, 3), 0).then_inc(ff_bank.h, 1)
                pe.wait_ge(dve_evac.h, dve_evac.at(layer, DVE_EVAC["FO"] + 7))
                ff_half(FO_B[0], range(4), 1).then_inc(ff_bank.h, 1)
                for k in range(2):
                    for n in FO_B[1:]:
                        if k == 0 and n == 7:
                            pe.wait_ge(dve_evac.h, dve_evac.at(layer, DVE_EVAC["FO"] + 8))
                        mm = ff_half(n, (k,), 1)
                    mm.then_inc(unit_done.h, 1)
                    if k == 0:
                        pe.wait_ge(dve_evac.h, dve_evac.at(layer, DVE_EVAC["FO"] + 9))
                        half_sum(layer, SQ["FO"] + 8, 0)
                for n in FO_B[1:]:
                    mm = ff_half(n, (2,), 1)
                    if n == FO_B[-1]:
                        mm.then_inc(unit_done.h, 1)
                    mm = ff_half(n, (3,), 1)
                    mm.then_inc(unit_done.h if n == FO_B[-1] else ff_bank.h, 1)

            half_sum(DEPTH, 0, 1, 0)

def _tiles(w, n0, n):
    k = w.shape[0] // P
    return w[:, n0:n0 + n * P].reshape(k, P, n, P).transpose(2, 1, 0, 3).reshape(n, P, k * P)


def _pairs(a, b):
    return np.stack([a, b], axis=1).reshape(-1, P, UC)


def _columns(v):
    return v.reshape(-1, P).T


def kernel(x, c, w_ada, b_ada, g_mix, w_in, b_in, sgu_ln_g, sgu_ln_b, sgu_w_s, sgu_b_s, w_pa, pool_w, pool_scale,
           w_pb, conv_w, conv_b, conv_ln_g, conv_ln_b, w_pc, w_out, g_ffn, w_ffn_in, w_ffn_out, g_final):
    import concourse.bacc as bacc
    from concourse import mybir as _mybir
    from concourse.bass_utils import run_bass_kernel_spmd as run

    (x, c, w_ada, b_ada, g_mix, w_in, b_in, sgu_ln_g, sgu_ln_b, sgu_w_s, sgu_b_s, w_pa, pool_w, pool_scale,
     w_pb, conv_w, conv_b, conv_ln_g, conv_ln_b, w_pc, w_out, g_ffn, w_ffn_in, w_ffn_out, g_final) = (
        np.asarray(a) for a in (x, c, w_ada, b_ada, g_mix, w_in, b_in, sgu_ln_g, sgu_ln_b, sgu_w_s, sgu_b_s, w_pa,
                                pool_w, pool_scale, w_pb, conv_w, conv_b, conv_ln_g, conv_ln_b, w_pc, w_out, g_ffn,
                                w_ffn_in, w_ffn_out, g_final))

    stream = []
    for l in range(DEPTH):
        wi = w_in[l]
        for half in range(2):
            v = wi[:, BT["v"] * P + half * 512:BT["v"] * P + half * 512 + 512]
            stream.append(v.reshape(4, 2, P, 512).transpose(0, 2, 1, 3).reshape(4, P, UC))
        stream.append(_pairs(_tiles(wi, BT["ag"] * P, 8), _tiles(wi, BT["a"] * P, 8)))
        stream.append(_tiles(wi, BT["u"] * P, 8))
        stream.append(_pairs(_tiles(wi, BT["gate"] * P, 8), _tiles(w_pa[l], 0, 8)))
        stream.append(_tiles(wi, BT["p"] * P, 8))
        stream.append(pool_w[l].reshape(2, 2, 2, P, 256).transpose(0, 3, 1, 2, 4).reshape(2, P, UC))
        stream.append(_pairs(_tiles(wi, (BT["gate"] + 8) * P, 8), _tiles(w_pb[l], 0, 8)))
        stream.append(_pairs(_tiles(wi, (BT["gate"] + 16) * P, 8), _tiles(w_pc[l], 0, 8)))
        stream.append(_tiles(w_out[l], 0, 8))
        stream.append(_pairs(_tiles(w_ffn_in[l], 0, FT), _tiles(w_ffn_in[l], D_FF, FT)))
        stream.append(w_ffn_out[l].reshape(FT, P, D))
    stream.append(stream[0][:RAW])
    weights = np.concatenate(stream)

    a = w_ada.reshape(DEPTH, 4, 2, P, 6, 2, 512).transpose(0, 4, 5, 1, 3, 2, 6).reshape(DEPTH, 6, 8, P, UC)
    b = b_ada.reshape(DEPTH, 6, D)
    order = [(0, 0), (0, 1)]
    for l in range(DEPTH):
        order += [(l, j) for j in range(2, 6)] + [((l + 1) % DEPTH, j) for j in (0, 1)]
    ada_stream = np.concatenate([a[l, j] for l, j in order])
    b_cols = np.concatenate([_columns(b[l, j]) for l, j in order], axis=1)

    cols = np.stack([np.concatenate([
        _columns(g_mix[l]), _columns(b_in[l]), _columns(g_ffn[l]), _columns(conv_b[l]), _columns(conv_ln_g[l]),
        _columns(conv_ln_b[l]), _columns(pool_scale[l]),
        conv_w[l].reshape(TAPS, CT, P).transpose(2, 1, 0).reshape(P, CT * TAPS)], axis=1) for l in range(DEPTH)])
    rows = np.concatenate([np.stack([b_in[l][BT["v"] * P:BT["v"] * P + D], sgu_ln_g[l], sgu_ln_b[l],
                                     sgu_b_s[l].reshape(-1)]) for l in range(DEPTH)])
    ws = sgu_w_s.transpose(0, 3, 1, 2).reshape(DEPTH, P, 8 * P)
    head = np.array([[win / min(t + 1, win) for t in range(WMAX)] for win in WINDOWS], np.float32).reshape(1, -1)
    f = np.float32
    fixed = np.concatenate([b_cols, _columns(g_final), _columns(c), np.full((P, 1), EPS, f), np.repeat(head, P, 0),
                            np.eye(P, dtype=f), np.ones((P, P), f), np.full((P, P), 1.0 / D, f)], axis=1)
    xT = x[0].reshape(S, CT, P).transpose(2, 1, 0).reshape(P, CT * S)

    nc = bacc.Bacc("TRN2", target_bir_lowering=False, num_devices=1, dynamic_dma_scratch_size=1024)
    arrays, args = {}, []
    for name, arr in (("xT", xT), ("fixed", fixed), ("cols", cols), ("rows", rows), ("ws", ws), ("w_ada", ada_stream),
                      ("weights", weights)):
        arrays[name + "_in"] = np.ascontiguousarray(arr)
        args.append(nc.dram_tensor(name + "_in", arr.shape, _mybir.dt.float32, kind="ExternalInput").ap())
    args.append(nc.dram_tensor("y_out", (P, CT * S), _mybir.dt.float32, kind="ExternalOutput").ap())
    trunk(nc, *args)
    r = run(nc, [arrays], core_ids=[0])
    y = r.results[0]["y_out"]
    return np.ascontiguousarray(y.reshape(P, CT, S).transpose(2, 1, 0).reshape(1, S, D))
```
